# Optimizing a Trainium2 kernel written in Bass

```python
import math
import jax, jax.numpy as jnp
from jax import lax
import numpy as np

D_MODEL = 2048
BATCH = 1
SEQ = 256
DEPTH = 1
DEC_BATCH = 8
DEC_SEQ = 8
PAST_LEN = 2048
PAGE_SIZE = 128

D_MIX = 2 * D_MODEL
D_SSM = D_MIX // 2
D_CONV = D_MIX - D_SSM
SSD_HEAD_DIM = 64
SSD_HEADS = D_SSM // SSD_HEAD_DIM
SSD_GROUPS = 4
SSD_REP = SSD_HEADS // SSD_GROUPS
SSD_STATE = 128
SSD_CONV_W = 4
SSD_CHUNK = 128
D_XBC = D_SSM + 2 * SSD_GROUPS * SSD_STATE
CONF_CONV_W = 31
D_FF = 4 * D_MODEL
Z_END = D_SSM
XBC_END = Z_END + D_XBC
DT_END = XBC_END + SSD_HEADS
N_IN = DT_END + 2 * D_CONV
EPS = 1e-6

kernel_name = "hymba_ssd_conformer_sandwich_decoder_step"

def rmsnorm(x, w):
    xf = x.astype(jnp.float32)
    r = lax.rsqrt(jnp.mean(xf * xf, axis=-1, keepdims=True) + EPS)
    return (xf * r).astype(x.dtype) * w

def layernorm(x, w, b):
    xf = x.astype(jnp.float32)
    mu = jnp.mean(xf, axis=-1, keepdims=True)
    var = jnp.mean(jnp.square(xf - mu), axis=-1, keepdims=True)
    return ((xf - mu) * lax.rsqrt(var + EPS)).astype(x.dtype) * w + b

def causal_depthwise_conv(u, buf, w, b):
    ext = jnp.concatenate([buf.astype(u.dtype), u], axis=1)
    ch = u.shape[-1]
    out = lax.conv_general_dilated(ext, w[:, None, :].astype(u.dtype), window_strides=(1,), padding='VALID',
                                   dimension_numbers=('NWC', 'WIO', 'NWC'), feature_group_count=ch)
    new_buf = ext[:, -(w.shape[0] - 1):]
    return out + b, new_buf

def ssd_scan(x, dt, A, B, C, h0):
    b, l = x.shape[:2]
    q = min(SSD_CHUNK, l)
    nc = -(-l // q)
    pad = nc * q - l
    if pad:
        padf = lambda a: jnp.pad(a, [(0, 0), (0, pad)] + [(0, 0)] * (a.ndim - 2))
        x, dt, B, C = padf(x), padf(dt), padf(B), padf(C)
    x = x.reshape(b, nc, q, *x.shape[2:])
    dt = dt.reshape(b, nc, q, *dt.shape[2:])
    B = B.reshape(b, nc, q, *B.shape[2:])
    C = C.reshape(b, nc, q, *C.shape[2:])
    cum = jnp.cumsum(dt * A, axis=2)
    causal = jnp.tril(jnp.ones((q, q), dtype=bool))[None, None, :, :, None, None]
    seg = cum[:, :, :, None] - cum[:, :, None, :]
    Lmat = jnp.exp(jnp.where(causal, seg, -jnp.inf))
    CB = jnp.einsum('bcign,bcjgn->bcijg', C, B)
    W = CB[..., None] * Lmat * dt[:, :, None]
    y_diag = jnp.einsum('bcijgr,bcjgrp->bcigrp', W, x)
    decay_to_end = jnp.exp(cum[:, :, -1:] - cum)
    chunk_states = jnp.einsum('bcjgn,bcjgr,bcjgrp->bcgrpn', B, decay_to_end * dt, x)
    chunk_decay = jnp.exp(cum[:, :, -1])

    def step(h, inp):
        d, s = inp
        return d[..., None, None] * h + s, h

    h_final, h_starts = lax.scan(step, h0, (jnp.moveaxis(chunk_decay, 1, 0), jnp.moveaxis(chunk_states, 1, 0)))
    h_starts = jnp.moveaxis(h_starts, 0, 1)
    y_off = jnp.einsum('bcign,bcgrpn->bcigrp', C, h_starts) * jnp.exp(cum)[..., None]
    y = (y_diag + y_off).reshape(b, nc * q, *x.shape[3:])[:, :l]
    return y, h_final

def mixer(u, h0, ssd_buf, conf_buf, w_in, ssd_conv_w, ssd_conv_b, dt_bias, a_log, d_skip, ssd_norm_w,
          conf_conv_w, conf_conv_b, conf_norm_w, conf_norm_b, w_out):
    b, l, _ = u.shape
    dtype = u.dtype
    proj = u @ w_in
    z = proj[..., :Z_END]
    xbc = proj[..., Z_END:XBC_END]
    dt_raw = proj[..., XBC_END:DT_END]
    glu = proj[..., DT_END:]
    xbc_c, new_ssd_buf = causal_depthwise_conv(xbc, ssd_buf, ssd_conv_w, ssd_conv_b)
    xbc_c = jax.nn.silu(xbc_c)
    xs = xbc_c[..., :D_SSM]
    Bm = xbc_c[..., D_SSM:D_SSM + SSD_GROUPS * SSD_STATE]
    Cm = xbc_c[..., D_SSM + SSD_GROUPS * SSD_STATE:]
    dt = jax.nn.softplus(dt_raw.astype(jnp.float32) + dt_bias.astype(jnp.float32))
    A = -jnp.exp(a_log.astype(jnp.float32))
    x5 = xs.astype(jnp.float32).reshape(b, l, SSD_GROUPS, SSD_REP, SSD_HEAD_DIM)
    y, h_new = ssd_scan(x5, dt.reshape(b, l, SSD_GROUPS, SSD_REP), A.reshape(SSD_GROUPS, SSD_REP),
                        Bm.astype(jnp.float32).reshape(b, l, SSD_GROUPS, SSD_STATE),
                        Cm.astype(jnp.float32).reshape(b, l, SSD_GROUPS, SSD_STATE),
                        h0.astype(jnp.float32).reshape(b, SSD_GROUPS, SSD_REP, SSD_HEAD_DIM, SSD_STATE))
    y = y + d_skip.astype(jnp.float32).reshape(SSD_GROUPS, SSD_REP)[..., None] * x5
    g = y.reshape(b, l, D_SSM) * jax.nn.silu(z.astype(jnp.float32))
    g = g.reshape(b, l, SSD_GROUPS, D_SSM // SSD_GROUPS)
    g = g * lax.rsqrt(jnp.mean(g * g, axis=-1, keepdims=True) + EPS)
    ssd_out = g.reshape(b, l, D_SSM).astype(dtype) * ssd_norm_w
    v = glu[..., :D_CONV] * jax.nn.sigmoid(glu[..., D_CONV:])
    vc, new_conf_buf = causal_depthwise_conv(v, conf_buf, conf_conv_w, conf_conv_b)
    conf_out = jax.nn.silu(layernorm(vc, conf_norm_w, conf_norm_b))
    mix = jnp.concatenate([ssd_out, conf_out], axis=-1) @ w_out
    h_new = h_new.reshape(b, SSD_HEADS, SSD_HEAD_DIM, SSD_STATE).astype(dtype)
    return mix, h_new, new_ssd_buf, new_conf_buf

def trunk(x, st_ssm, st_ssd_conv, st_conf, w_in, ssd_conv_w, ssd_conv_b, dt_bias, a_log, d_skip, ssd_norm_w,
          conf_conv_w, conf_conv_b, conf_norm_w, conf_norm_b, w_out, norm_pre_mix, norm_post_mix,
          norm_pre_mlp, norm_post_mlp, w_up, w_down):
    new_ssm, new_sc, new_cc = [], [], []
    for i in range(DEPTH):
        mix, h_new, sbuf, cbuf = mixer(rmsnorm(x, norm_pre_mix[i]), st_ssm[i], st_ssd_conv[i], st_conf[i],
                                       w_in[i], ssd_conv_w[i], ssd_conv_b[i], dt_bias[i], a_log[i], d_skip[i],
                                       ssd_norm_w[i], conf_conv_w[i], conf_conv_b[i], conf_norm_w[i],
                                       conf_norm_b[i], w_out[i])
        x = x + rmsnorm(mix, norm_post_mix[i])
        hid = jnp.square(jax.nn.relu(rmsnorm(x, norm_pre_mlp[i]) @ w_up[i]))
        x = x + rmsnorm(hid @ w_down[i], norm_post_mlp[i])
        new_ssm.append(h_new)
        new_sc.append(sbuf)
        new_cc.append(cbuf)
    return x, jnp.stack(new_ssm), jnp.stack(new_sc), jnp.stack(new_cc)

def setup_inputs(seed: int = 0) -> dict:
    key = jax.random.key(seed)
    ks = jax.random.split(key, 24)
    nrm = lambda k, s, sc: jax.random.normal(k, s, jnp.float32) * sc
    dt0 = jnp.exp(jax.random.uniform(ks[8], (DEPTH, SSD_HEADS), jnp.float32) * (math.log(0.1) - math.log(0.001)) + math.log(0.001))
    dt_bias = dt0 + jnp.log(-jnp.expm1(-dt0))
    a_log = jnp.log(jax.random.uniform(ks[9], (DEPTH, SSD_HEADS), jnp.float32, 1.0, 16.0))
    return {
        "x_prompt": nrm(ks[0], (BATCH, SEQ, D_MODEL), 1.0),
        "x_sample": nrm(ks[1], (DEC_BATCH, DEC_SEQ, D_MODEL), 1.0),
        "state_ssm": nrm(ks[2], (DEPTH, DEC_BATCH, SSD_HEADS, SSD_HEAD_DIM, SSD_STATE), 0.3),
        "state_ssd_conv": nrm(ks[3], (DEPTH, DEC_BATCH, SSD_CONV_W - 1, D_XBC), 1.0),
        "state_conformer_conv": nrm(ks[4], (DEPTH, DEC_BATCH, CONF_CONV_W - 1, D_CONV), 0.5),
        "w_in": nrm(ks[5], (DEPTH, D_MODEL, N_IN), D_MODEL ** -0.5),
        "ssd_conv_w": nrm(ks[6], (DEPTH, SSD_CONV_W, D_XBC), SSD_CONV_W ** -0.5),
        "ssd_conv_b": nrm(ks[7], (DEPTH, D_XBC), 0.02),
        "dt_bias": dt_bias,
        "a_log": a_log,
        "d_skip": 1.0 + nrm(ks[10], (DEPTH, SSD_HEADS), 0.1),
        "ssd_norm_w": 1.0 + nrm(ks[11], (DEPTH, D_SSM), 0.05),
        "conf_conv_w": nrm(ks[12], (DEPTH, CONF_CONV_W, D_CONV), CONF_CONV_W ** -0.5),
        "conf_conv_b": nrm(ks[13], (DEPTH, D_CONV), 0.02),
        "conf_norm_w": 1.0 + nrm(ks[14], (DEPTH, D_CONV), 0.05),
        "conf_norm_b": nrm(ks[15], (DEPTH, D_CONV), 0.02),
        "w_out": nrm(ks[16], (DEPTH, D_MIX, D_MODEL), D_MIX ** -0.5),
        "norm_pre_mix": 1.0 + nrm(ks[17], (DEPTH, D_MODEL), 0.05),
        "norm_post_mix": 1.0 + nrm(ks[18], (DEPTH, D_MODEL), 0.05),
        "norm_pre_mlp": 1.0 + nrm(ks[19], (DEPTH, D_MODEL), 0.05),
        "norm_post_mlp": 1.0 + nrm(ks[20], (DEPTH, D_MODEL), 0.05),
        "w_up": nrm(ks[21], (DEPTH, D_MODEL, D_FF), D_MODEL ** -0.5),
        "w_down": nrm(ks[22], (DEPTH, D_FF, D_MODEL), D_FF ** -0.5),
    }

def reference(x_prompt, x_sample, state_ssm, state_ssd_conv, state_conformer_conv, w_in, ssd_conv_w, ssd_conv_b,
              dt_bias, a_log, d_skip, ssd_norm_w, conf_conv_w, conf_conv_b, conf_norm_w, conf_norm_b, w_out,
              norm_pre_mix, norm_post_mix, norm_pre_mlp, norm_post_mlp, w_up, w_down):
    weights = (w_in, ssd_conv_w, ssd_conv_b, dt_bias, a_log, d_skip, ssd_norm_w, conf_conv_w, conf_conv_b,
               conf_norm_w, conf_norm_b, w_out, norm_pre_mix, norm_post_mix, norm_pre_mlp, norm_post_mlp,
               w_up, w_down)
    dt_p = x_prompt.dtype
    b = x_prompt.shape[0]
    zero_ssm = jnp.zeros((DEPTH, b, SSD_HEADS, SSD_HEAD_DIM, SSD_STATE), dt_p)
    zero_sc = jnp.zeros((DEPTH, b, SSD_CONV_W - 1, D_XBC), dt_p)
    zero_cc = jnp.zeros((DEPTH, b, CONF_CONV_W - 1, D_CONV), dt_p)
    y_prompt, p_ssm, p_sc, p_cc = trunk(x_prompt, zero_ssm, zero_sc, zero_cc, *weights)
    y_sample, s_ssm, s_sc, s_cc = trunk(x_sample, state_ssm, state_ssd_conv, state_conformer_conv, *weights)
    return (y_prompt, y_sample, p_ssm, p_sc, p_cc, s_ssm, s_sc, s_cc)


_drawn_inputs = setup_inputs


def setup_inputs(seed=0):
    import zlib

    import numpy as np

    out = dict(_drawn_inputs(seed))
    spreads = {}
    factors = {'conf_conv_b': 3.335, 'conf_norm_b': 6.93}
    for name, (base, spread) in spreads.items():
        noise = np.random.default_rng([zlib.crc32(name.encode()), seed]).standard_normal(out[name].shape)
        drawn = base * np.exp(spread * noise) if base else spread * noise
        out[name] = __import__('jax').numpy.asarray(drawn.astype(out[name].dtype))
    for name, factor in factors.items():
        out[name] = (out[name] * factor).astype(out[name].dtype)
    return out
```

```python
from contextlib import ExitStack

import numpy as np

import concourse.bass as bass
from concourse import mybir

F32 = mybir.dt.float32
F32R = mybir.dt.float32r
BF16 = mybir.dt.bfloat16
ALU = mybir.AluOpType
ACT = mybir.ActivationFunctionType
ds = bass.ds

P = 128
D = 2048
NT = D // P
SEQ = 256
NB, DS = 8, 8
TOK = SEQ + NB * DS
HEADS, HD, GROUPS, STATE = 32, 64, 4, 128
D_XBC = D + 2 * GROUPS * STATE
NX = D_XBC // P
TAPS, XTAPS = 31, 4
HALO, XHALO = TAPS - 1, XTAPS - 1
D_FF = 4 * D
COL_Z, COL_XBC, COL_DT, COL_GLU = 0, D, D + D_XBC, D + D_XBC + HEADS
EPS = 1e-6
MASKED = -1.0e30

PEXT = HALO + SEQ
SEXT = HALO + DS
VLEN = PEXT + NB * SEXT
XPEXT = XHALO + SEQ
XSEXT = XHALO + DS
XLEN = XPEXT + NB * XSEXT
VNEW = HALO + NB * DS
XNEW = XHALO + NB * XHALO

R_CONV, R_CB, R_NW, R_NB, R_SSD, R_PREMIX, R_POSTMIX, R_PREMLP, R_POSTMLP, R_XW, R_XB, R_DSKIP = (
    1, 32, 33, 34, 35, 36, 37, 38, 39, 40, 44, 0)
NROW = 45

Q_DT, Q_GLU, Q_XBC, Q_Z, Q_WC, Q_WS, Q_MLP = 0, 1, 17, 29, 37, 45, 53
Q_END = Q_MLP + 4 * 16


def q_up(q):
    return Q_MLP + 16 * q


def q_down(q):
    return Q_MLP + 16 * q + 8


class Steps:

    def __init__(self, sem):
        self.sem, self.at, self.made = sem, 0, 0

    def inc(self, ins):
        ins.then_inc(self.sem, 1)
        self.at = self.at + 1
        self.made += 1
        return self.at

    def enter(self, i, first, per):
        self.top, self.per, self.first = self.at, per, first
        self.at = (i - first) * per + self.top
        self.made = 0

    def leave(self, turns):
        assert self.made == self.per, (self.made, self.per)
        self.at = self.top + turns * self.per


def build(nc, x_prompt, x_sample, state_ssm, state_ssd_conv, state_conf, w_in, ssd_conv_w, ssd_conv_b,
          dt_bias, a_log, d_skip, ssd_norm_w, conf_conv_w, conf_conv_b, conf_norm_w, conf_norm_b, w_out,
          norm_pre_mix, norm_post_mix, norm_pre_mlp, norm_post_mlp, w_up, w_down,
          y_prompt, y_sample, p_ssm, p_sc, p_cc, s_ssm, s_sc, s_cc, xt_dram):
    with ExitStack() as ctx:
        def sem(name):
            return ctx.enter_context(nc.semaphore(name))

        slab = ctx.enter_context(nc.sbuf_tensor("slab", [P, 53200], F32, align_bytes=64))
        base = (int(nc.sbuf_base) - 53200 * 4)
        cursor = [0]

        def place(name, shape, dt=F32, at=None):
            size = int(np.prod(shape[1:])) * (2 if dt == BF16 else 4)
            size = -(-size // 32) * 8
            off = cursor[0] if at is None else at
            if at is None:
                cursor[0] += size
            assert off + size <= 53200, (name, off, size)
            return nc.alloc_sbuf_tensor_at(name, shape, dt, offset=base + 4 * off)

        a_off = 0
        ahi = place("ahi", [P, NT, TOK], F32R)
        alo = place("alo", [P, NT, TOK], F32R)
        raw = place("raw", [P, 4, 4, 256])
        whi = place("whi", [P, 4, 4, 256], F32R)
        wlo = place("wlo", [P, 4, 4, 256], F32R)
        ar = cursor[0]
        cursor[0] += 22240
        vx = place("vx", [P, NT, VLEN], at=ar)
        xb = place("xb", [P, NX, TOK], at=ar + NT * VLEN)
        zg = place("zg", [P, NT, TOK], at=ar + NT * VLEN + NX * TOK)
        xn = place("xn", [P, 3, D], at=ar)
        xt0 = place("xt0", [P, NT, TOK], at=ar + 6144)
        cst = place("cst", [4 * HALO, 2, D], at=ar + 11264)
        sst = place("sst", [NB * XHALO, D_XBC], at=ar + 15360)
        prow = place("prow", [NROW, D], at=ar + 18432)
        prow2 = place("prow2", [XTAPS + 1, D_XBC - D], at=ar + 20480)
        mix = place("mix", [P, NT, TOK], at=ar)
        sc = ar + 5120
        bt = place("bt", [P, TOK], at=sc)
        xst = place("xst", [P, TOK], at=sc + 320)
        btok = place("btok", [P, 3, P], at=sc + 640)
        bm = place("bm", [P, NB, P], at=sc + 1024)
        xd = place("xd", [P, 3, P], at=sc + 2048)
        xdd = place("xdd", [P, 3, P], at=sc + 2432)
        h0t = place("h0t", [P, NB, P], at=sc + 2816)
        pst = place("pst", [P, P], at=sc + 3840)
        s0s = place("s0s", [P, P], at=sc + 3968)
        yoff = place("yoff", [P, 192], at=sc + 4096)
        xr = place("xr", [P, NT, TOK], at=ar + NT * VLEN)
        hhi = place("hhi", [P, NT, TOK], F32R, at=ar + 5120)
        hlo = place("hlo", [P, NT, TOK], F32R, at=ar + 10240)
        ya = place("ya", [P, NT, TOK], at=ar + 15360)
        yo = place("yo", [P, 3, D], at=a_off)
        par = place("par", [P, NT, NROW])
        sw = place("sw", [P, NX, XTAPS + 1])
        ident = place("ident", [P, P])
        identb = place("identb", [P, P], BF16)
        ones = place("ones", [P, P])
        mneg = place("mneg", [P, TOK], BF16)
        sel = place("sel", [P, HEADS], BF16)
        nsel = place("nsel", [P, HEADS], BF16)
        cum3 = place("cum3", [P, TOK], BF16)
        ecum3 = place("ecum3", [P, TOK], BF16)
        tcol = place("tcol", [P, 3, 96])
        blk = place("blk", [P, NB])
        rb = place("rb", [P, TOK])
        eps = place("eps", [P, 1])
        dcol = place("dcol", [HEADS, 2])
        selt = place("selt", [P, 2, HD], BF16)
        sm = cursor[0]
        xs = place("xs", [P, NX, NB * XHALO])
        xe = place("xe", [P, 2, 2, XLEN])
        vst = place("vst", [P, 2, VNEW])
        vtok = place("vtok", [VNEW, 256])
        xw = place("xw", [P, 2, 2, XNEW])
        xtok = place("xtok", [XNEW, 512])
        vacc = place("vacc", [P, TOK])
        sg = place("sg", [P, 2, TOK])
        msum = place("msum", [P, TOK])
        sqb = place("sqb", [P, 4, TOK])
        t1 = place("t1", [P, 2, TOK], at=sm + 4320)
        ss = place("ss", [P, 4], at=sm + 4960)
        diag = place("diag", [P, 3, P], at=sm + 4968)
        dsk = place("dsk", [1, HEADS], at=sm)
        hw = place("hw", [HEADS, 8, TOK], at=ar + 18432)
        hst = place("hst", [96, TOK], at=ar + 18432 + 8 * TOK)
        hb = place("hb", [HEADS, 3, TOK], BF16, at=ar + 18432 + 9 * TOK)
        wgt = place("wgt", [P, 2, TOK], at=sm)
        h0 = place("h0", [P, 2, NB, P], at=sm + 640)
        hout = place("hout", [P, NB, P], at=sm + 2688)
        ecb = place("ecb", [P, 192], at=sm + 3712)
        hts = place("hts", [P, P], at=sm + 3904)
        ysum = place("ysum", [P, TOK], at=sm + 4032)
        gss = place("gss", [P, GROUPS, TOK], at=sm + 4352)
        sqp = place("sqp", [P, TOK], at=sm + 5632)
        sq2 = place("sq2", [P, 2, TOK], at=sm)
        acc2 = place("acc2", [P, 2, TOK], at=sm + 640)
        rh = place("rh", [P, 2, TOK], at=sm + 1280)
        hs = place("hs", [P, 2, TOK], at=sm + 1920)
        t4 = place("t4", [P, 4, TOK], at=sm + 2560)
        rb2 = place("rb2", [P, TOK], at=sm + 3840)
        ps = ctx.enter_context(nc.psum_tensor("ps", [P, 8, 512], F32))

        raw_ready = [sem(f"raw_ready{s}") for s in range(4)]
        hi_done, lo_done, weights_used = sem("hi_done"), sem("lo_done"), sem("weights_used")
        ahi_done, act_ready = sem("ahi_done"), sem("act_ready")
        read_act, read_dve = sem("read_act"), sem("read_dve")
        pool_turn = sem("pool_turn")
        act_step, dve_step, pool_step = sem("act_step"), sem("dve_step"), sem("pool_step")
        x_in = [sem(f"x_in{c}") for c in range(3)]
        dsk_in = sem("dsk_in")
        par_in, cst_in, sst_in, dcol_in = sem("par_in"), sem("cst_in"), sem("sst_in"), sem("dcol_in")
        consts = sem("consts")
        x_trans, x_copied, t1_done = sem("x_trans"), sem("x_copied"), sem("t1_done")
        par_trans, par_done = sem("par_trans"), sem("par_done")
        rms_root, diag_done, rb_mm, rb_done = sem("rms_root"), sem("diag_done"), sem("rb_mm"), sem("rb_done")
        cst_trans, cst_done, sst_trans, sst_done = (
            sem("cst_trans"), sem("cst_done"), sem("sst_trans"), sem("sst_done"))
        xt_stored, halo_zero = sem("xt_stored"), sem("halo_zero")
        dt_act, dt_dve, dt_trans, dt_ready = sem("dt_act"), sem("dt_dve"), sem("dt_trans"), sem("dt_ready")
        vst_ready, vt_done, vtok_ready, vout = (
            sem("vst_ready"), sem("vt_done"), sem("vtok_ready"), sem("vout"))
        conv_turn, msum_done = sem("conv_turn"), sem("msum_done")
        xconv_done, xb_done, xw_ready, xwt_done, xtok_ready, xout = (
            sem("xconv_done"), sem("xb_done"), sem("xw_ready"), sem("xwt_done"), sem("xtok_ready"), sem("xout"))
        mean_mm, mean_done, cent_done, sq_ready, sq_used, var_root, cn_done, silu_done = (
            sem("mean_mm"), sem("mean_done"), sem("cent_done"), sem("sq_ready"), sem("sq_used"),
            sem("var_root"), sem("cn_done"), sem("silu_done"))
        bt_ready, bt_trans, btok_ready, bm_ready, cb_done = (
            sem("bt_ready"), sem("bt_trans"), sem("btok_ready"), sem("bm_ready"), sem("cb_done"))
        xst_ready, xtile_trans, xd_ready, seg_done, exp_done, mixw_done = (
            sem("xst_ready"), sem("xtile_trans"), sem("xd_ready"), sem("seg_done"), sem("exp_done"),
            sem("mixw_done"))
        h0_in = [sem("h0_in0"), sem("h0_in1")]
        h0_trans, h0t_ready, pstart_done, hts_ready = (
            sem("h0_trans"), sem("h0t_ready"), sem("pstart_done"), sem("hts_ready"))
        selt_ready = sem("selt_ready")
        ecb_mm, ecb_ready, st_done, hnew_done, pst_done, y_done, y_read, g_done = (
            sem("ecb_mm"), sem("ecb_ready"), sem("st_done"), sem("hnew_done"), sem("pst_done"),
            sem("y_done"), sem("y_read"), sem("g_done"))
        hout_out, pst_out = sem("hout_out"), sem("pst_out")
        gss_done, gn_mm, gn_root, gn_done = sem("gss_done"), sem("gn_mm"), sem("gn_root"), sem("gn_done")
        xr_in, acc_done, rms_mm, root2, rb2_done, t4_done, x1_done = (
            sem("xr_in"), sem("acc_done"), sem("rms_mm"), sem("root2"), sem("rb2_done"), sem("t4_done"),
            sem("x1_done"))
        rh_done, hs_done, hhi_done, hid_ready = sem("rh_done"), sem("hs_done"), sem("hhi_done"), sem("hid_ready")
        ot_trans, ot_copied, y_out, old_rows = sem("ot_trans"), sem("ot_copied"), sem("y_out"), sem("old_rows")

        def rows(w, r0):
            return w[ds(r0, D), :].rearrange("(k p) n -> p k n", p=P)

        w_in2, w_out2, w_up2, w_down2 = w_in[0], w_out[0], w_up[0], w_down[0]
        in_k, ssd_k, conf_k, up_k = rows(w_in2, 0), rows(w_out2, 0), rows(w_out2, D), rows(w_up2, 0)
        down_k = w_down2.rearrange("(q k p) n -> p q k n", p=P, k=NT)

        def v_prompt(t, n, lo, hi):
            return vx[:, ds(t, n), lo:hi]

        def v_sample(t, n, lo, hi):
            return vx[:, ds(t, n), PEXT:VLEN].rearrange("p n (b j) -> p n b j", b=NB)[:, :, :, lo:hi]

        def v_sample1(t, lo, hi):
            return vx[:, t, PEXT:VLEN].rearrange("p (b j) -> p b j", b=NB)[:, :, lo:hi]

        def seqs(ap):
            return ap.rearrange("p (b j) -> p b j", b=NB)

        def gemm_bank(p):
            return ps[:, 2 * p:2 * p + 2, 0:TOK]

        block = ctx.enter_context(nc.Block())

        @block.sync
        def _(sp):
            for c in range(2):
                sp.dma_start(xn[:, c, :], x_prompt[0, c * P:(c + 1) * P, :]).then_inc(x_in[c], 16)
            sp.dma_start(xn[0:NB * DS, 2, :], x_sample.rearrange("b s d -> (b s) d")).then_inc(x_in[2], 16)

            def load(src, pair, kq, width=256):
                if isinstance(pair, int) and pair == 0:
                    pass
                else:
                    sp.wait_ge(lo_done, 4 * pair + kq - 3)
                sp.dma_start(raw[:, kq, :, 0:width], src).then_inc(raw_ready[kq], 16)

            for kq in range(4):
                load(in_k[:, 4 * kq:4 * kq + 4, COL_DT:COL_DT + P], Q_DT, kq, P)

            def body(mat, pair0, cols, i):
                for p in range(2):
                    for kq in range(4):
                        load(mat[:, 4 * kq:4 * kq + 4, ds(cols[p] , 256)], pair0 + 2 * i + p, kq)

            with sp.Fori(0, 8) as i:
                body(in_k, Q_GLU, (COL_GLU + D + 256 * i, COL_GLU + 256 * i), i)
            with sp.Fori(0, 6) as i:
                body(in_k, Q_XBC, (COL_XBC + 512 * i, COL_XBC + 512 * i + 256), i)
            with sp.Fori(0, 4) as i:
                body(in_k, Q_Z, (COL_Z + 512 * i, COL_Z + 512 * i + 256), i)
            with sp.Fori(0, 4) as i:
                body(conf_k, Q_WC, (512 * i, 512 * i + 256), i)
            with sp.Fori(0, 4) as i:
                body(ssd_k, Q_WS, (512 * i, 512 * i + 256), i)
            with sp.Fori(0, 4) as q:
                with sp.Fori(0, 4) as i:
                    body(up_k, q_up(q), (D * q + 512 * i, D * q + 512 * i + 256), i)
                with sp.Fori(0, 4) as i:
                    for p in range(2):
                        for kq in range(4):
                            load(down_k[:, q, 4 * kq:4 * kq + 4, ds(512 * i + 256 * p, 256)],
                                 q_down(q) + 2 * i + p, kq)

        @block.gpsimd
        def _(pool):
            st = Steps(pool_step)
            pool.dma_start(prow[R_CONV:R_CONV + TAPS, :], conf_conv_w[0]).then_inc(par_in, 16)
            for r, w in ((R_CB, conf_conv_b), (R_NW, conf_norm_w), (R_NB, conf_norm_b), (R_SSD, ssd_norm_w),
                         (R_PREMIX, norm_pre_mix), (R_POSTMIX, norm_post_mix), (R_PREMLP, norm_pre_mlp),
                         (R_POSTMLP, norm_post_mlp)):
                pool.dma_start(prow[r:r + 1, :], w).then_inc(par_in, 16)
            pool.dma_start(prow[R_XW:R_XW + XTAPS, :], ssd_conv_w[0, :, 0:D]).then_inc(par_in, 16)
            pool.dma_start(prow[R_XB:R_XB + 1, :], ssd_conv_b[:, 0:D]).then_inc(par_in, 16)
            pool.dma_start(dsk[:], d_skip).then_inc(dsk_in, 16)
            pool.dma_start(prow2[0:XTAPS, :], ssd_conv_w[0, :, D:D_XBC]).then_inc(par_in, 16)
            pool.dma_start(prow2[XTAPS:XTAPS + 1, :], ssd_conv_b[:, D:D_XBC]).then_inc(par_in, 16)

            pool.wait_ge(dsk_in, 16)
            pool.tensor_copy(prow[R_DSKIP:R_DSKIP + 1, :].rearrange("a (h p) -> a h p", p=HD),
                             dsk[:].unsqueeze(2).to_broadcast([1, HEADS, HD]))

            pool.memset(ident[:], 0.0)
            pool.memset(identb[:], 0.0)
            pool.memset(ones[:], 1.0)
            pool.memset(mneg[:], 0.0)
            pool.memset(sel[:], 0.0)
            pool.memset(nsel[:], 0.0)
            pool.memset(eps[:], EPS)
            pool.memset(ss[:], 1.0)
            pool.memset(cum3[:], 0.0)
            pool.memset(ecum3[:], 0.0)
            v = st.inc(pool.memset(blk[:], 1.0))
            pool.wait_ge(pool_step, v)
            for m in (ident, identb):
                pool.affine_select(out=m[:], in_=m[:], compare_op=ALU.not_equal, fill=1.0, base=0,
                                   pattern=[[-1, P]], channel_multiplier=1).then_inc(consts, 1)
            for c in range(2):
                half = mneg[:, c * P:(c + 1) * P]
                pool.affine_select(out=half, in_=half, compare_op=ALU.is_ge, fill=MASKED, base=0,
                                   pattern=[[1, P]], channel_multiplier=-1)
            third = seqs(mneg[:, SEQ:TOK])
            v = st.inc(pool.affine_select(out=third, in_=third, compare_op=ALU.is_ge, fill=MASKED, base=64,
                                          pattern=[[DS, NB], [1, DS]], channel_multiplier=-1))
            pool.wait_ge(pool_step, v)
            pool.affine_select(out=third, in_=third, compare_op=ALU.is_ge, fill=MASKED, base=-64,
                               pattern=[[-DS, NB], [0, DS]], channel_multiplier=1)
            for m, one in ((sel, 1.0), (nsel, -1.0)):
                for part in range(3):
                    v = st.inc(pool.affine_select(out=m[:], in_=m[:], compare_op=ALU.not_equal, fill=one,
                                                  base=-HEADS * part, pattern=[[-1, HEADS]],
                                                  channel_multiplier=1))
                    pool.wait_ge(pool_step, v)
            v = st.inc(pool.affine_select(out=blk[:], in_=blk[:], compare_op=ALU.is_ge, fill=0.0, base=-64,
                                          pattern=[[-DS, NB]], channel_multiplier=1))
            pool.wait_ge(pool_step, v)
            pool.affine_select(out=blk[:], in_=blk[:], compare_op=ALU.is_ge, fill=0.0, base=64 + DS - 1,
                               pattern=[[DS, NB]], channel_multiplier=-1).then_inc(consts, 1)

            for h in range(2):
                pool.dma_start(cst[:, h, :], state_conf[0, 4 * h:4 * h + 4].rearrange("b j d -> (b j) d")
                               ).then_inc(cst_in, 16)
            pool.dma_start(sst[:], state_ssd_conv[0].rearrange("b j d -> (b j) d")).then_inc(sst_in, 16)
            pool.dma_start(dcol[:, 0:1], dt_bias.rearrange("o h -> h o")).then_inc(dcol_in, 16)
            pool.dma_start(dcol[:, 1:2], a_log.rearrange("o h -> h o")).then_inc(dcol_in, 16)
            pool.dma_start(s_cc[0, :, 0:HALO - DS, :], state_conf[0, :, DS:HALO, :]).then_inc(old_rows, 16)

            pool.memset(xe[:, :, :, 0:XHALO], 0.0)
            pool.memset(msum[:], 0.0)
            pool.wait_ge(x_trans, NT)
            pool.wait_ge(xt_stored, 16)
            pool.memset(vx[:, :, 0:HALO], 0.0).then_inc(halo_zero, 1)

            def plain():
                pool.sem_inc(pool_turn, 1)

            def gather_v(i):
                pool.wait_ge(read_dve, i + 1)
                if not (isinstance(i, int) and i == 0):
                    pool.wait_ge(vt_done, i)
                plain()
                pool.tensor_copy(vst[:, :, 0:HALO], v_prompt(2 * i, 2, SEQ, PEXT))
                for n in range(2):
                    last = pool.tensor_copy(seqs(vst[:, n, HALO:VNEW]), v_sample1(2 * i + n, HALO, SEXT))
                last.then_inc(vst_ready, 1)

            def store_v(i):
                pool.wait_ge(vtok_ready, i + 1)
                pool.dma_start(p_cc[0, 0, :, ds(256 * i, 256)], vtok[0:HALO, :]).then_inc(vout, 16)
                pool.dma_start(s_cc[0, :, HALO - DS:HALO, ds(256 * i, 256)], vtok[HALO:VNEW, :]
                               ).then_inc(vout, 16)

            def sum_tile(j):
                pool.wait_ge(conv_turn, j + 2)
                pool.wait_ge(pool_step, st.at)
                plain()
                pool.tensor_tensor(msum[:, 0:SEQ], msum[:, 0:SEQ], vx[:, j, 0:SEQ], ALU.add)
                st.inc(pool.tensor_tensor(seqs(msum[:, SEQ:TOK]), seqs(msum[:, SEQ:TOK]),
                                          v_sample1(j, 0, DS), ALU.add))

            gather_v(0)
            with pool.Fori(1, 8) as i:
                st.enter(i, 1, 1)
                store_v(i - 1)
                sum_tile(i - 1)
                gather_v(i)
                st.leave(7)
            store_v(7)

            def gather_x(i, p):
                pool.wait_ge(read_act, 8 + 2 * i + p + 1)
                if p == 0 and not (isinstance(i, int) and i == 0):
                    pool.wait_ge(xwt_done, i)
                plain()
                pool.tensor_copy(xw[:, p, :, 0:XHALO], xe[:, p, :, XPEXT - XHALO:XPEXT])
                for n in range(2):
                    last = pool.tensor_copy(
                        seqs(xw[:, p, n, XHALO:XNEW]), seqs(xe[:, p, n, XPEXT:XLEN])[:, :, XSEXT - XHALO:XSEXT])
                last.then_inc(xw_ready, 1)

            def store_x(i):
                pool.wait_ge(xtok_ready, i + 1)
                pool.dma_start(p_sc[0, 0, :, ds(512 * i, 512)], xtok[0:XHALO, :]).then_inc(xout, 16)
                pool.dma_start(s_sc[0].rearrange("b j d -> (b j) d")[:, ds(512 * i, 512)], xtok[XHALO:XNEW, :]
                               ).then_inc(xout, 16)

            gather_x(0, 0)
            gather_x(0, 1)
            sum_tile(7)
            with pool.Fori(1, 6) as i:
                st.enter(i, 1, 1)
                gather_x(i, 0)
                store_x(i - 1)
                gather_x(i, 1)
                sum_tile(7 + i)
                st.leave(5)
            store_x(5)
            for j in range(13, 16):
                sum_tile(j)
            pool.wait_ge(pool_step, st.at)
            pool.sem_inc(msum_done, 1)

            def square_tile(i, j):
                pool.wait_ge(g_done, 4 * i + j + 1)
                plain()
                g = zg[:, 4 * i + j, :]
                if j == 0:
                    st.inc(pool.tensor_tensor(gss[:, i, :], g, g, ALU.mult))
                    return
                v = st.inc(pool.tensor_tensor(sqp[:], g, g, ALU.mult))
                pool.wait_ge(pool_step, v)
                plain()
                st.inc(pool.tensor_tensor(gss[:, i, :], gss[:, i, :], sqp[:], ALU.add))
                pool.wait_ge(pool_step, st.at)
                plain()

            pool.wait_ge(act_ready, 2 * NT)
            with pool.Fori(0, 4) as i:
                st.enter(i, 0, 7)
                for j in range(4):
                    pool.tensor_copy(selt[:], sel[:, ds(8 * i + 2 * j, 2)].unsqueeze(2).to_broadcast([P, 2, HD])
                                     ).then_inc(selt_ready, 1)
                    square_tile(i, j)
                st.leave(4)
            pool.wait_ge(pool_step, st.at)
            pool.sem_inc(gss_done, 1)
            pool.wait_ge(y_done, NT)
            pool.wait_ge(xst_ready, NT + 1)
            pool.wait_ge(bt_ready, GROUPS + 1)
            pool.dma_start(xr[:], xt_dram.rearrange("p (t n) -> p t n", t=NT)).then_inc(xr_in, 16)
            pool.wait_ge(hout_out, 16 * NT)
            v = st.inc(pool.memset(acc2[:], 0.0))
            pool.wait_ge(pool_step, v)

            def square_pair(t0):
                plain()
                v = st.inc(pool.tensor_tensor(sq2[:], mix[:, ds(t0, 2), :], mix[:, ds(t0, 2), :], ALU.mult))
                pool.wait_ge(pool_step, v)
                plain()
                v = st.inc(pool.tensor_tensor(acc2[:], acc2[:], sq2[:], ALU.add))
                pool.wait_ge(pool_step, v)

            with pool.Fori(0, 8) as r:
                st.enter(r, 0, 2)
                pool.wait_ge(read_dve, 8 + r + 1)
                square_pair(2 * r)
                st.leave(8)
            pool.sem_inc(acc_done, 1)
            pool.wait_ge(rms_mm, 1)
            pool.wait_ge(acc_done, 1)
            v = st.inc(pool.memset(acc2[:], 0.0))
            pool.wait_ge(pool_step, v)
            for r in range(8):
                pool.wait_ge(x1_done, 2 * r + 2)
                square_pair(2 * r)
            pool.sem_inc(acc_done, 1)
            pool.wait_ge(rms_mm, 2)
            pool.wait_ge(acc_done, 2)
            v = st.inc(pool.memset(acc2[:], 0.0))
            pool.wait_ge(pool_step, v)
            for r in range(8):
                pool.wait_ge(read_dve, 32 + r + 1)
                v = st.inc(pool.tensor_tensor(sq2[:], ya[:, 2 * r:2 * r + 2, :], ya[:, 2 * r:2 * r + 2, :],
                                              ALU.mult))
                pool.wait_ge(pool_step, v)
                v = st.inc(pool.tensor_tensor(acc2[:], acc2[:], sq2[:], ALU.add))
                pool.wait_ge(pool_step, v)
            pool.sem_inc(acc_done, 1)
            pool.wait_ge(old_rows, 16)
            pool.wait_ge(vout, 2 * 16 * 8)
            pool.wait_ge(xout, 2 * 16 * 6)

        @block.scalar
        def _(act):
            st = Steps(act_step)

            def split(pair, kq, width=256):
                act.wait_ge(raw_ready[kq], 16 * (pair + 1))
                if not (isinstance(pair, int) and pair == 0):
                    act.wait_ge(weights_used, 4 * pair + kq - 3)
                act.activation(whi[:, kq, :, 0:width], raw[:, kq, :, 0:width], ACT.Copy).then_inc(hi_done, 1)

            def ahead(pair0, i, c):
                split(pair0 + 2 * i + (c + 2) // 4, (c + 2) % 4)

            act.wait_ge(consts, 3)
            for c in range(3):
                n = P if c < 2 else NB * DS
                junk = xt0[0:n, :, :].rearrange("p a b -> p (a b)")[:, 0:D]
                act.wait_ge(x_in[c], 16)
                if c:
                    act.wait_ge(act_step, st.at)
                st.inc(act.activation(junk, xn[0:n, c, :], ACT.Square, accum_out=ss[0:n, c:c + 1]))
            act.wait_ge(act_step, st.at)
            act.activation(ss[:, 0:3], ss[:, 0:3], ACT.Sqrt, bias=eps[:, 0:1], scale=1.0 / D
                           ).then_inc(rms_root, 1)
            act.wait_ge(par_trans, 1)
            act.activation(par[:, 0:8, :], ps[:, 5, 0:8 * NROW].rearrange("p (t r) -> p t r", t=8), ACT.Copy)
            act.activation(par[:, 8:16, :], ps[:, 6, 0:8 * NROW].rearrange("p (t r) -> p t r", t=8), ACT.Copy)
            v = st.inc(act.activation(sw[:, NT:NX, :], ps[:, 6, 360:400].rearrange("p (t r) -> p t r", t=8),
                                      ACT.Copy))
            act.wait_ge(act_step, v)
            act.activation(sw[:, 0:NT, :], par[:, :, R_XW:R_XB + 1], ACT.Copy).then_inc(par_done, 1)
            act.wait_ge(rb_mm, 1)
            act.activation(rb[:], ps[:, 4, 0:TOK], ACT.Copy).then_inc(rb_done, 1)
            split(Q_DT, 0, P)
            split(Q_DT, 1, P)
            act.wait_ge(par_done, 1)
            for t in range(NT):
                act.wait_ge(x_trans, t + 1)
                act.activation(xt0[:, t, :], ps[:, t % 4, 0:TOK], ACT.Copy).then_inc(x_copied, 1)
                act.wait_ge(t1_done, t + 1)
                act.activation(ahi[:, t, :], t1[:, t % 2, :], ACT.Copy, scale=par[:, t, R_PREMIX:R_PREMIX + 1]
                               ).then_inc(ahi_done, 1)
            act.wait_ge(x_copied, NT)
            act.dma_start(xt_dram.rearrange("p (t n) -> p t n", t=NT), xt0[:]).then_inc(xt_stored, 16)
            split(Q_DT, 2, P)
            split(Q_DT, 3, P)
            split(Q_GLU, 0)
            split(Q_GLU, 1)

            def conv_states(batch):
                act.wait_ge(xt_stored, 16)
                for t in range(4 * batch, 4 * batch + 4):
                    act.wait_ge(cst_trans, t + 1)
                    act.activation(v_sample1(t, 0, HALO), ps[:, 6 + t % 2, 0:NB * HALO].rearrange(
                        "p (b j) -> p b j", b=NB), ACT.Copy).then_inc(cst_done, 1)

            def xconv_states():
                act.wait_ge(sst_trans, 1)
                act.activation(xs[:, 0:12, :], ps[:, 7, 0:288].rearrange("p (t r) -> p t r", t=12), ACT.Copy)
                act.activation(xs[:, 12:24, :], ps[:, 5, 0:288].rearrange("p (t r) -> p t r", t=12), ACT.Copy
                               ).then_inc(sst_done, 1)

            def dt_part(c):
                if c == 0:
                    act.wait_ge(weights_used, 4)
                    act.wait_ge(dcol_in, 32)
                    act.activation(hw[:, 0, :], ps[0:HEADS, 4, 0:TOK], ACT.Identity, bias=dcol[:, 0:1]
                                   ).then_inc(dt_act, 1)
                if c == 1:
                    act.wait_ge(dt_dve, 1)
                    act.activation(hw[:, 1, :], hw[:, 2, :], ACT.Exp, scale=-1.0)
                    act.activation(dcol[:, 1:2], dcol[:, 1:2], ACT.Exp).then_inc(dt_act, 1)
                if c == 3:
                    act.wait_ge(dt_dve, 2)
                    act.activation(hw[:, 6, :], hw[:, 5, :], ACT.Exp)
                    act.activation(hw[:, 7, :], hw[:, 4, :], ACT.Exp).then_inc(dt_act, 1)
                if c == 7:
                    act.wait_ge(dt_trans, 1)
                    act.activation(tcol[:], ps[:, 4, 0:288].rearrange("p (c r) -> p c r", c=3), ACT.Copy
                                   ).then_inc(dt_ready, 1)

            def sigmoid(i):
                act.wait_ge(weights_used, 4 * (Q_GLU + 2 * i) + 4)
                if not (isinstance(i, int) and i == 0):
                    act.wait_ge(read_dve, i)
                act.activation(sg[:], gemm_bank(0), ACT.Sigmoid).then_inc(read_act, 1)

            def v_rows(i):
                act.wait_ge(vt_done, i + 1)
                if not (isinstance(i, int) and i == 0):
                    act.wait_ge(vout, 32 * i)
                act.activation(vtok[:], ps[0:VNEW, 5, 0:256], ACT.Copy).then_inc(vtok_ready, 1)

            def glu(i):
                for c in range(8):
                    ahead(Q_GLU, i, c)
                    if isinstance(i, int) and i == 0:
                        dt_part(c)
                        if 1 <= c <= 4:
                            conv_states(c - 1)
                        if c == 5:
                            xconv_states()
                    if c == 3:
                        sigmoid(i)
                    if c == 5 and not (isinstance(i, int) and i == 0):
                        v_rows(i - 1)

            glu(0)
            with act.Fori(1, 8) as i:
                glu(i)

            def xbc_evac(i, p):
                r = 2 * i + p
                act.wait_ge(weights_used, 4 * (Q_XBC + r) + 4)
                if not (isinstance(i, int) and i == 0):
                    act.wait_ge(xconv_done, r - 1)
                    act.wait_ge(xw_ready, r - 1)
                buf = xe[:, p, :, XPEXT:XLEN].rearrange("p n (b j) -> p n b j", b=NB)
                act.activation(buf[:, :, :, 0:XHALO],
                               xs[:, ds(4 * i + 2 * p, 2), :].rearrange("p n (b j) -> p n b j", b=NB), ACT.Copy)
                act.activation(xe[:, p, :, XHALO:XPEXT], ps[:, 2 * p:2 * p + 2, 0:SEQ], ACT.Copy)
                act.activation(buf[:, :, :, XHALO:XSEXT],
                               ps[:, 2 * p:2 * p + 2, SEQ:TOK].rearrange("p n (b j) -> p n b j", b=NB),
                               ACT.Copy).then_inc(read_act, 1)

            def xbc_silu(i, p):
                act.wait_ge(xconv_done, 2 * i + p + 1)
                t = xb[:, ds(4 * i + 2 * p, 2), :]
                act.activation(t, t, ACT.Silu).then_inc(xb_done, 1)

            def x_rows(i):
                act.wait_ge(xwt_done, i + 1)
                if not (isinstance(i, int) and i == 0):
                    act.wait_ge(xout, 32 * i)
                act.activation(xtok[:], ps[0:XNEW, 5, :], ACT.Copy).then_inc(xtok_ready, 1)

            def xbc(i):
                first = isinstance(i, int) and i == 0
                for c in range(8):
                    ahead(Q_XBC, i, c)
                    if c == 1 and not first:
                        xbc_silu(i - 1, 1)
                    if c == 3:
                        xbc_evac(i, 0)
                    if c == 5:
                        xbc_silu(i, 0)
                        if first:
                            v_rows(7)
                        else:
                            x_rows(i - 1)
                    if c == 7:
                        xbc_evac(i, 1)

            act.wait_ge(sst_done, 1)
            xbc(0)
            with act.Fori(1, 6) as i:
                xbc(i)

            def z_silu(i, p):
                act.wait_ge(weights_used, 4 * (Q_Z + 2 * i + p) + 4)
                act.activation(zg[:, ds(4 * i + 2 * p, 2), :], gemm_bank(p), ACT.Silu).then_inc(read_act, 1)

            def z(i):
                for c in range(8):
                    ahead(Q_Z, i, c)
                    if isinstance(i, int) and i == 0 and c == 1:
                        xbc_silu(5, 1)
                    if isinstance(i, int) and i == 0 and c == 5:
                        x_rows(5)
                    if c == 3:
                        z_silu(i, 0)
                    if c == 7:
                        z_silu(i, 1)

            def square_group(gg):
                act.wait_ge(cent_done, gg + 1)
                if gg:
                    act.wait_ge(sq_used, gg)
                act.activation(sqb[:, :, 0:SEQ], v_prompt(4 * gg, 4, 0, SEQ), ACT.Square)
                for n in range(4):
                    last = act.activation(seqs(sqb[:, n, SEQ:TOK]), v_sample1(4 * gg + n, 0, DS), ACT.Square)
                last.then_inc(sq_ready, 1)

            z(0)
            with act.Fori(1, 3) as i:
                z(i)
            for c in range(8):
                ahead(Q_Z, 3, c)
                if c == 1:
                    act.wait_ge(mean_mm, 1)
                    act.activation(rb[:], ps[:, 4, 0:TOK], ACT.Copy, scale=1.0 / D).then_inc(mean_done, 1)
                if c == 3:
                    z_silu(3, 0)
                if c >= 4:
                    square_group(c - 4)
            z_silu(3, 1)

            act.wait_ge(sq_used, 4)
            act.wait_ge(cent_done, 4)
            act.activation(rb[:], ps[:, 4, 0:TOK], ACT.Sqrt, bias=eps[:, 0:1], scale=1.0 / D).then_inc(var_root, 1)

            def conf_silu(t):
                w, b = par[:, t, R_NW:R_NW + 1], par[:, t, R_NB:R_NB + 1]
                act.wait_ge(cn_done, t // 4 + 1)
                act.activation(vx[:, t, 0:SEQ], vx[:, t, 0:SEQ], ACT.Silu, bias=b, scale=w)
                act.activation(v_sample1(t, 0, DS), v_sample1(t, 0, DS), ACT.Silu, bias=b, scale=w
                               ).then_inc(silu_done, 1)

            def conf_hi(t):
                act.wait_ge(silu_done, t + 1)
                if t == 0:
                    act.wait_ge(weights_used, 4 * Q_WC)
                act.activation(ahi[:, t, 0:SEQ], vx[:, t, 0:SEQ], ACT.Copy)
                act.activation(seqs(ahi[:, t, SEQ:TOK]), v_sample1(t, 0, DS), ACT.Copy).then_inc(ahi_done, 1)

            conf_silu(0)
            for t in range(1, NT):
                conf_silu(t)
                conf_hi(t - 1)
            conf_hi(NT - 1)

            def stage_x(T):
                if not (isinstance(T, int) and T == 0):
                    act.wait_ge(xtile_trans, T)
                act.activation(xst[:], xb[:, T, :], ACT.Copy).then_inc(xst_ready, 1)

            def stage_b(i):
                if not (isinstance(i, int) and i == 0):
                    act.wait_ge(cb_done, i)
                act.activation(bt[:], xb[:, NT + i, :], ACT.Copy).then_inc(bt_ready, 1)

            def load_h0(T, slot):
                act.dma_start(h0[:, slot], state_ssm[0].rearrange("b (t e) p n -> (e p) t b n", e=2)[:, T]
                              ).then_inc(h0_in[slot], 16)

            def store_h(T):
                act.wait_ge(hnew_done, T + 1)
                act.dma_start(s_ssm[0].rearrange("b (t e) p n -> (e p) t b n", e=2)[:, T], hout[:]
                              ).then_inc(hout_out, 16)
                act.wait_ge(pst_done, T + 1)
                act.dma_start(p_ssm[0, 0].rearrange("(t e) p n -> (e p) t n", e=2)[:, T], pst[:]
                              ).then_inc(pst_out, 16)

            def wc(i, final=False):
                for j in range(4):
                    T = 4 * i + j
                    first = isinstance(i, int) and i == 0 and j == 0
                    ahead(Q_WC, i, 2 * j)
                    if j == 0:
                        act.wait_ge(bt_trans, i + 1)
                        act.activation(btok[:], ps[:, 4, 0:384].rearrange("p (c n) -> p c n", c=3), ACT.Copy
                                       ).then_inc(btok_ready, 1)
                    act.wait_ge(seg_done, 2 * T + 1)
                    if not first:
                        act.wait_ge(y_done, T)
                    act.activation(wgt[:, 0, :], ps[:, 3, 0:TOK], ACT.Exp).then_inc(exp_done, 1)
                    act.wait_ge(h0_trans, T + 1)
                    act.activation(h0t[:, 0:4, :], ps[:, 6, :].rearrange("p (b n) -> p b n", b=4), ACT.Copy)
                    act.activation(h0t[:, 4:8, :], ps[:, 7, :].rearrange("p (b n) -> p b n", b=4), ACT.Copy
                                   ).then_inc(h0t_ready, 1)
                    act.wait_ge(pstart_done, T + 1)
                    act.activation(hts[:], ps[:, 4, 384:512], ACT.Copy).then_inc(hts_ready, 1)
                    if not first:
                        act.wait_ge(hnew_done, T)
                    if not (final and j == 3):
                        load_h0(T + 1, (j + 1) % 2)
                    ahead(Q_WC, i, 2 * j + 1)
                    act.wait_ge(ecb_mm, T + 1)
                    if not first:
                        act.wait_ge(y_read, T)
                    act.activation(ecb[:], ps[:, 2, TOK:512], ACT.Copy).then_inc(ecb_ready, 1)
                    act.wait_ge(seg_done, 2 * T + 2)
                    act.activation(wgt[:, 1, :], ps[:, 3, 0:TOK], ACT.Exp).then_inc(exp_done, 1)
                    if j % 2:
                        p = j // 2
                        act.wait_ge(weights_used, 4 * (Q_WC + 2 * i + p) + 4)
                        act.activation(mix[:, ds(4 * i + 2 * p, 2), :], gemm_bank(0), ACT.Copy
                                       ).then_inc(read_act, 1)
                    if j == 3:
                        stage_b(i + 1)
                    stage_x(T + 1)
                    store_h(T)

            act.wait_ge(act_ready, 2 * NT)
            act.wait_ge(dt_ready, 1)
            act.wait_ge(xb_done, 12)
            stage_b(0)
            stage_x(0)
            act.wait_ge(sq_used, 4)
            act.wait_ge(msum_done, 1)
            act.wait_ge(vout, 2 * 16 * 8)
            act.wait_ge(xout, 2 * 16 * 6)
            load_h0(0, 0)
            wc(0)
            with act.Fori(1, 3) as i:
                wc(i)
            wc(3, final=True)

            act.wait_ge(gn_mm, 1)
            act.activation(gss[:], ps[:, 2:6, 0:TOK], ACT.Sqrt, bias=eps[:, 0:1], scale=GROUPS / D
                           ).then_inc(gn_root, 1)
            for t in range(NT):
                act.wait_ge(gn_done, t // 4 + 1)
                act.wait_ge(weights_used, 4 * Q_WS)
                act.activation(ahi[:, t, :], zg[:, t, :], ACT.Copy, scale=par[:, t, R_SSD:R_SSD + 1]
                               ).then_inc(ahi_done, 1)

            with act.Fori(0, 4) as i:
                for c in range(8):
                    ahead(Q_WS, i, c)

            act.wait_ge(rms_mm, 1)
            act.activation(rb[:], ps[:, 4, 0:TOK], ACT.Sqrt, bias=eps[:, 0:1], scale=1.0 / D).then_inc(root2, 1)
            for t in range(NT):
                act.wait_ge(x1_done, t + 1)
                act.activation(ahi[:, t, :], mix[:, t, :], ACT.Copy, scale=par[:, t, R_PREMLP:R_PREMLP + 1]
                               ).then_inc(ahi_done, 1)

            act.wait_ge(hout_out, 16 * NT)
            act.wait_ge(pst_out, 16 * NT)

            def up(q, i, start=False):
                for c in range(8):
                    ahead(q_up(q), i, c)
                    if start and c == 1:
                        act.wait_ge(rms_mm, 2)
                        act.activation(rb2[:], ps[:, 5, 0:TOK], ACT.Sqrt, bias=eps[:, 0:1], scale=1.0 / D
                                       ).then_inc(root2, 1)
                    if c % 4 == 3:
                        p = c // 4
                        n = 8 * q + 2 * i + p
                        act.wait_ge(rh_done, n + 1)
                        act.activation(hs[:], rh[:], ACT.Square).then_inc(hs_done, 1)
                        act.wait_ge(hs_done, n + 1)
                        act.activation(hhi[:, ds(4 * i + 2 * p, 2), :], hs[:], ACT.Copy).then_inc(hhi_done, 1)

            def down(q, i, last=False):
                for c in range(8):
                    if not (last and c >= 6):
                        ahead(q_down(q), i, c)
                    if c % 4 == 3 and isinstance(q, int) and q == 0:
                        p = c // 4
                        act.wait_ge(weights_used, 4 * (q_down(q) + 2 * i + p) + 4)
                        act.activation(ya[:, ds(4 * i + 2 * p, 2), :], gemm_bank(p), ACT.Copy
                                       ).then_inc(read_act, 1)

            up(0, 0, start=True)
            with act.Fori(1, 4) as i:
                up(0, i)
            with act.Fori(0, 4) as i:
                down(0, i)
            with act.Fori(1, 3) as q:
                with act.Fori(0, 4) as i:
                    up(q, i)
                with act.Fori(0, 4) as i:
                    down(q, i)
            with act.Fori(0, 4) as i:
                up(3, i)
            with act.Fori(0, 3) as i:
                down(3, i)
            down(3, 3, last=True)

            act.wait_ge(rms_mm, 3)
            act.activation(rb[:], ps[:, 4, 0:TOK], ACT.Sqrt, bias=eps[:, 0:1], scale=1.0 / D).then_inc(root2, 1)
            for g in range(4):
                act.wait_ge(ot_trans, g + 1)
                b = 3 * (g % 2)
                act.activation(yo[:, 0:2, 512 * g:512 * g + 512], ps[:, b:b + 2, :], ACT.Copy)
                act.activation(yo[0:NB * DS, 2, 512 * g:512 * g + 512], ps[0:NB * DS, b + 2, :], ACT.Copy
                               ).then_inc(ot_copied, 1)
                act.wait_ge(ot_copied, g + 1)
                col = slice(512 * g, 512 * g + 512)
                act.dma_start(y_prompt[0].rearrange("(c p) d -> p c d", p=P)[:, :, col], yo[:, 0:2, col]
                              ).then_inc(y_out, 16)
                act.dma_start(y_sample.rearrange("b s d -> (b s) d")[:, col], yo[0:NB * DS, 2, col]
                              ).then_inc(y_out, 16)
            act.wait_ge(xt_stored, 16)
            act.wait_ge(hout_out, 16 * NT)
            act.wait_ge(pst_out, 16 * NT)
            act.wait_ge(y_out, 2 * 16 * 4)

        @block.vector
        def _(dve):
            st = Steps(dve_step)

            def split(pair, kq, width=256):
                dve.wait_ge(hi_done, 4 * pair + kq + 1)
                dve.tensor_tensor(wlo[:, kq, :, 0:width], raw[:, kq, :, 0:width],
                                  whi[:, kq, :, 0:width].bitcast(F32), ALU.subtract).then_inc(lo_done, 1)

            def ahead(pair0, i, c):
                split(pair0 + 2 * i + (c + 2) // 4, (c + 2) % 4)

            dve.memset(vacc[:], 0.0).then_inc(conv_turn, 1)
            dve.wait_ge(rms_root, 1)
            dve.wait_ge(consts, 3)
            v = st.inc(dve.reciprocal(ss[:, 0:3], ss[:, 0:3]))
            dve.wait_ge(dve_step, v)
            for c in range(3):
                last = dve.tensor_scalar(diag[:, c, :], ident[:], ss[:, c:c + 1], None, ALU.mult)
            last.then_inc(diag_done, 1)
            split(Q_DT, 0, P)
            split(Q_DT, 1, P)

            def in_lo(t):
                dve.wait_ge(ahi_done, t + 1)
                dve.scalar_tensor_tensor(out=alo[:, t, :], in0=t1[:, t % 2, :],
                                         scalar=par[:, t, R_PREMIX:R_PREMIX + 1],
                                         in1=ahi[:, t, :].bitcast(F32), op0=ALU.mult, op1=ALU.subtract
                                         ).then_inc(act_ready, 1)

            dve.wait_ge(rb_done, 1)
            dve.wait_ge(par_done, 1)
            for t in range(NT):
                dve.wait_ge(x_copied, t + 1)
                if t >= 2:
                    dve.wait_ge(act_ready, t - 1)
                dve.tensor_tensor(t1[:, t % 2, :], ps[:, t % 4, 0:TOK], rb[:], ALU.mult).then_inc(t1_done, 1)
                if t:
                    in_lo(t - 1)
            in_lo(NT - 1)
            split(Q_DT, 2, P)
            split(Q_DT, 3, P)
            split(Q_GLU, 0)
            split(Q_GLU, 1)

            def chain(ins):
                dve.wait_ge(dve_step, st.inc(ins))

            X, E, A, S2, CUM, DL, DTE, ECUM = range(8)

            def row(r):
                return hw[:, r, :]

            def dt_part(c):
                if c == 0:
                    dve.wait_ge(dt_act, 1)
                    chain(dve.scalar_tensor_tensor(out=row(A), in0=row(X), scalar=-1.0, in1=row(X),
                                                   op0=ALU.mult, op1=ALU.max))
                    dve.tensor_scalar(row(DTE), row(X), 0.0, None, ALU.max)
                    dve.memset(row(CUM), 1.0).then_inc(dt_dve, 1)
                    dve.wait_ge(dt_dve, 1)
                    for k in range(2):
                        dve.memset(hw[:, CUM, k * P:k * P + 1], 0.0)
                    chain(dve.memset(seqs(hw[:, CUM, SEQ:TOK])[:, :, 0:1], 0.0))
                if c == 1:
                    dve.wait_ge(dt_act, 2)
                    chain(dve.tensor_scalar(row(A), row(E), 2.0, None, ALU.add))
                    chain(dve.reciprocal(row(A), row(A)))
                    chain(dve.tensor_tensor(row(E), row(E), row(A), ALU.mult))
                    chain(dve.tensor_tensor(row(S2), row(E), row(E), ALU.mult))
                    chain(dve.tensor_scalar(row(A), row(S2), 1.0 / 17.0, None, ALU.mult))
                if c == 2:
                    for n in (15, 13, 11, 9, 7, 5, 3):
                        chain(dve.scalar_tensor_tensor(out=row(A), in0=row(A), scalar=1.0 / n, in1=row(S2),
                                                       op0=ALU.add, op1=ALU.mult))
                if c == 3:
                    chain(dve.scalar_tensor_tensor(out=row(A), in0=row(A), scalar=1.0, in1=row(E),
                                                   op0=ALU.add, op1=ALU.mult))
                    chain(dve.scalar_tensor_tensor(out=row(X), in0=row(A), scalar=2.0, in1=row(DTE),
                                                   op0=ALU.mult, op1=ALU.add))
                    chain(dve.tensor_scalar(row(A), row(X), dcol[:, 1:2], -1.0, ALU.mult, ALU.mult))
                    chain(dve.tensor_tensor_scan(out=row(E), data0=row(CUM), data1=row(A), initial=0.0,
                                                 op0=ALU.mult, op1=ALU.add))
                    dve.tensor_copy(row(CUM), row(E))
                    for k in range(2):
                        dve.tensor_tensor(hw[:, DL, k * P:(k + 1) * P],
                                          hw[:, E, k * P + P - 1:k * P + P].to_broadcast([HEADS, P]),
                                          hw[:, E, k * P:(k + 1) * P], ALU.subtract)
                    dve.tensor_tensor(seqs(hw[:, DL, SEQ:TOK]),
                                      seqs(hw[:, E, SEQ:TOK])[:, :, DS - 1:DS].to_broadcast([HEADS, NB, DS]),
                                      seqs(hw[:, E, SEQ:TOK]), ALU.subtract).then_inc(dt_dve, 1)
                if c == 4:
                    dve.wait_ge(dt_act, 3)
                    dve.wait_ge(dt_dve, 2)
                    chain(dve.tensor_tensor(row(DTE), row(DTE), row(X), ALU.mult))
                    dve.tensor_copy(hst[0:32, :], row(E))
                    dve.tensor_copy(hst[32:64, :], row(X))
                    dve.tensor_copy(hst[64:96, :], row(DTE)).then_inc(dt_dve, 1)
                if c in (5, 6):
                    r, dst = ((E, cum3), (ECUM, ecum3))[c - 5]
                    if c == 5:
                        dve.wait_ge(dt_dve, 3)
                    chain(dve.tensor_copy(hb[:, 0, :], row(r)))
                    chain(dve.tensor_tensor(row(r), row(r), hb[:, 0, :], ALU.subtract))
                    chain(dve.tensor_copy(hb[:, 1, :], row(r)))
                    chain(dve.tensor_tensor(row(r), row(r), hb[:, 1, :], ALU.subtract))
                    chain(dve.tensor_copy(hb[:, 2, :], row(r)))
                    for part in range(3):
                        last = dve.tensor_copy(dst[32 * part:32 * part + 32, :], hb[:, part, :])
                    chain(last)

            def make_v(i):
                dve.wait_ge(weights_used, 4 * (Q_GLU + 2 * i + 1) + 4)
                dve.wait_ge(read_act, i + 1)
                dve.tensor_tensor(v_prompt(2 * i, 2, HALO, PEXT), ps[:, 2:4, 0:SEQ], sg[:, :, 0:SEQ], ALU.mult)
                for n in range(2):
                    last = dve.tensor_tensor(v_sample1(2 * i + n, HALO, SEXT), seqs(ps[:, 2 + n, SEQ:TOK]),
                                             seqs(sg[:, n, SEQ:TOK]), ALU.mult)
                last.then_inc(read_dve, 1)
                dve.wait_ge(read_dve, i + 1)

            CUTS = [31, 27, 23, 19, 15, 11, 7, 3, 0]
            tap_at = [0, 0]

            def conv(j, c):
                acc = (vacc[:, 0:SEQ], seqs(vacc[:, SEQ:TOK]))
                if c == 0:
                    dve.wait_ge(conv_turn, j + 1)
                for k in range(CUTS[c] - 1, CUTS[c + 1] - 1, -1):
                    w = par[:, j, R_CONV + k:R_CONV + k + 1]
                    src = (vx[:, j, k:k + SEQ], v_sample1(j, k, k + DS))
                    out = acc if k else src
                    for s in range(2):
                        if k == TAPS - 1:
                            ins = dve.tensor_scalar(acc[s], src[s], w, par[:, j, R_CB:R_CB + 1],
                                                    ALU.mult, ALU.add)
                        else:
                            dve.wait_ge(dve_step, tap_at[s])
                            ins = dve.scalar_tensor_tensor(out=out[s], in0=src[s], scalar=w, in1=acc[s],
                                                           op0=ALU.mult, op1=ALU.add)
                        if k == 0 and s == 1:
                            ins.then_inc(conv_turn, 1)
                        else:
                            tap_at[s] = st.inc(ins)

            CONV_STEPS = 2 * TAPS - 1

            def glu(i):
                for c in range(8):
                    ahead(Q_GLU, i, c)
                    if isinstance(i, int) and i == 0:
                        dt_part(c)
                        if c == 7:
                            dve.wait_ge(halo_zero, 1)
                            dve.wait_ge(cst_done, NT)
                    else:
                        conv(i - 1, c)
                    if c == 7:
                        make_v(i)

            glu(0)
            with dve.Fori(1, 8) as i:
                st.enter(i, 1, CONV_STEPS)
                glu(i)
                st.leave(7)

            def xconv(i, p):
                dve.wait_ge(read_act, 8 + 2 * i + p + 1)
                last_at = [0] * 4
                for k in range(XTAPS - 1, -1, -1):
                    for n in range(2):
                        t = 4 * i + 2 * p + n
                        src = (xe[:, p, n, k:k + SEQ], seqs(xe[:, p, n, XPEXT:XLEN])[:, :, k:k + DS])
                        dst = (xb[:, t, 0:SEQ], seqs(xb[:, t, SEQ:TOK]))
                        w = sw[:, t, k:k + 1]
                        for s in range(2):
                            if k == XTAPS - 1:
                                ins = dve.tensor_scalar(dst[s], src[s], w, sw[:, t, XTAPS:XTAPS + 1],
                                                        ALU.mult, ALU.add)
                            else:
                                dve.wait_ge(dve_step, last_at[2 * n + s])
                                ins = dve.scalar_tensor_tensor(out=dst[s], in0=src[s], scalar=w, in1=dst[s],
                                                               op0=ALU.mult, op1=ALU.add)
                            if k == 0 and n == 1 and s == 1:
                                ins.then_inc(xconv_done, 1)
                            else:
                                last_at[2 * n + s] = st.inc(ins)

            XCONV_STEPS = 4 * XTAPS - 1

            def xbc(i):
                for c in range(8):
                    ahead(Q_XBC, i, c)
                    conv(7 + i, c)
                    if c == 3:
                        xconv(i, 0)
                    if c == 7:
                        xconv(i, 1)

            xbc(0)
            with dve.Fori(1, 6) as i:
                st.enter(i, 1, CONV_STEPS + 2 * XCONV_STEPS)
                xbc(i)
                st.leave(5)

            def z(i):
                for c in range(8):
                    ahead(Q_Z, i, c)
                    conv(13 + i, c)

            z(0)
            with dve.Fori(1, 3) as i:
                st.enter(i, 1, CONV_STEPS)
                z(i)
                st.leave(2)

            def on_group(gg, op, sem_, chained):
                m = rb[:, 0:SEQ].unsqueeze(1).to_broadcast([P, 4, SEQ])
                dve.tensor_tensor(v_prompt(4 * gg, 4, 0, SEQ), v_prompt(4 * gg, 4, 0, SEQ), m, op)
                for n in range(4):
                    v = v_sample1(4 * gg + n, 0, DS)
                    last = dve.tensor_tensor(v, v, seqs(rb[:, SEQ:TOK]), op)
                last.then_inc(sem_, 1)

            for c in range(8):
                ahead(Q_Z, 3, c)
                if c == 1:
                    dve.wait_ge(mean_done, 1)
                    dve.wait_ge(conv_turn, NT + 1)
                    dve.wait_ge(msum_done, 1)
                    for gg in range(4):
                        on_group(gg, ALU.subtract, cent_done, False)
            dve.wait_ge(var_root, 1)
            v = st.inc(dve.reciprocal(rb[:], rb[:]))
            dve.wait_ge(dve_step, v)
            dve.wait_ge(sq_ready, 4)
            for gg in range(4):
                on_group(gg, ALU.mult, cn_done, True)
            for t in range(NT):
                dve.wait_ge(ahi_done, NT + t + 1)
                dve.tensor_tensor(alo[:, t, 0:SEQ], vx[:, t, 0:SEQ], ahi[:, t, 0:SEQ].bitcast(F32), ALU.subtract)
                dve.tensor_tensor(seqs(alo[:, t, SEQ:TOK]), v_sample1(t, 0, DS),
                                  seqs(ahi[:, t, SEQ:TOK].bitcast(F32)), ALU.subtract).then_inc(act_ready, 1)

            xt3 = ps[:, 4, 0:384].rearrange("p (c h d) -> p c h d", c=3, h=2)

            def wc(i):
                for j in range(4):
                    T = 4 * i + j
                    first = isinstance(i, int) and i == 0 and j == 0
                    ahead(Q_WC, i, 2 * j)
                    if j == 0:
                        dve.wait_ge(btok_ready, i + 1)
                        if not (isinstance(i, int) and i == 0):
                            dve.wait_ge(st_done, 4 * i)
                        dve.tensor_tensor(bm[:], btok[:, 2, :].unsqueeze(1).to_broadcast([P, NB, P]),
                                          blk[:].unsqueeze(2).to_broadcast([P, NB, P]), ALU.mult
                                          ).then_inc(bm_ready, 1)
                    dve.wait_ge(xtile_trans, T + 1)
                    if not first:
                        dve.wait_ge(y_done, T)
                    dve.tensor_tensor(xd[:].rearrange("p c (h d) -> p c h d", h=2), xt3,
                                      tcol[:, :, ds(HEADS + 2 * T, 2)].unsqueeze(3).to_broadcast([P, 3, 2, HD]),
                                      ALU.mult)
                    dve.tensor_tensor(xdd[:].rearrange("p c (h d) -> p c h d", h=2), xt3,
                                      tcol[:, :, ds(2 * HEADS + 2 * T, 2)].unsqueeze(3).to_broadcast([P, 3, 2, HD]),
                                      ALU.mult).then_inc(xd_ready, 1)
                    if j == 0:
                        dve.wait_ge(cb_done, i + 1)
                    dve.wait_ge(exp_done, 2 * T + 1)
                    dve.tensor_tensor(wgt[:, 0, :], ps[:, 2, 0:TOK], wgt[:, 0, :], ALU.mult).then_inc(mixw_done, 1)
                    ahead(Q_WC, i, 2 * j + 1)
                    dve.wait_ge(exp_done, 2 * T + 2)
                    dve.tensor_tensor(wgt[:, 1, :], ps[:, 2, 0:TOK], wgt[:, 1, :], ALU.mult).then_inc(mixw_done, 1)
                    dve.wait_ge(st_done, T + 1)
                    dve.wait_ge(ecb_ready, T + 1)
                    if not first:
                        dve.wait_ge(hout_out, 16 * T)
                        dve.wait_ge(pst_out, 16 * T)
                    for b in range(NB):
                        col = P + DS * b + DS - 1
                        last = dve.scalar_tensor_tensor(
                            out=hout[:, b, :], in0=h0[:, j % 2, b, :], scalar=ecb[:, col:col + 1],
                            in1=ps[:, 6 + b // 4, (b % 4) * P:(b % 4 + 1) * P], op0=ALU.mult, op1=ALU.add)
                    last.then_inc(hnew_done, 1)
                    v = st.inc(dve.tensor_scalar(s0s[:], ps[:, 4, 0:P], ecb[:, P - 1:P], None, ALU.mult))
                    dve.wait_ge(dve_step, v)
                    dve.tensor_tensor(pst[:], ps[:, 4, P:2 * P], s0s[:], ALU.add).then_inc(pst_done, 1)
                    dve.wait_ge(y_done, T + 1)
                    v1 = st.inc(dve.tensor_tensor(yoff[:], ps[:, 5, TOK:512], ecb[:], ALU.mult))
                    v2 = st.inc(dve.scalar_tensor_tensor(
                        out=ysum[:], in0=xb[:, T, :], scalar=par[:, T, R_DSKIP:R_DSKIP + 1],
                        in1=ps[:, 5, 0:TOK], op0=ALU.mult, op1=ALU.add))
                    dve.wait_ge(dve_step, v2)
                    dve.tensor_tensor(ysum[:, P:TOK], ysum[:, P:TOK], yoff[:], ALU.add).then_inc(y_read, 1)
                    dve.wait_ge(y_read, T + 1)
                    dve.tensor_tensor(zg[:, T, :], ysum[:], zg[:, T, :], ALU.mult).then_inc(g_done, 1)
                    dve.wait_ge(g_done, T + 1)

            WC_STEPS = 4 * 3
            dve.wait_ge(act_ready, 2 * NT)
            dve.wait_ge(dt_ready, 1)
            dve.wait_ge(read_act, 28)
            wc(0)
            with dve.Fori(1, 4) as i:
                st.enter(i, 1, WC_STEPS)
                wc(i)
                st.leave(3)

            dve.wait_ge(gn_root, 1)
            for g in range(GROUPS):
                v = st.inc(dve.reciprocal(gss[:, g, :], gss[:, g, :]))
                dve.wait_ge(dve_step, v)
                dve.tensor_tensor(zg[:, 4 * g:4 * g + 4, :], zg[:, 4 * g:4 * g + 4, :],
                                  gss[:, g, :].unsqueeze(1).to_broadcast([P, 4, TOK]), ALU.mult
                                  ).then_inc(gn_done, 1)
            for t in range(NT):
                dve.wait_ge(ahi_done, 2 * NT + t + 1)
                dve.scalar_tensor_tensor(out=alo[:, t, :], in0=zg[:, t, :], scalar=par[:, t, R_SSD:R_SSD + 1],
                                         in1=ahi[:, t, :].bitcast(F32), op0=ALU.mult, op1=ALU.subtract
                                         ).then_inc(act_ready, 1)

            with dve.Fori(0, 4) as i:
                for c in range(8):
                    ahead(Q_WS, i, c)
                    if c % 4 == 3:
                        p = c // 4
                        dve.wait_ge(weights_used, 4 * (Q_WS + 2 * i + p) + 4)
                        m = mix[:, ds(4 * i + 2 * p, 2), :]
                        dve.tensor_tensor(m, gemm_bank(p), m, ALU.add).then_inc(read_dve, 1)

            dve.wait_ge(root2, 1)
            v = st.inc(dve.reciprocal(rb[:], rb[:]))
            dve.wait_ge(dve_step, v)
            dve.wait_ge(xr_in, 16)
            dve.wait_ge(read_dve, 16)
            dve.wait_ge(hout_out, 16 * NT)
            for g in range(4):
                if g:
                    dve.wait_ge(x1_done, 4 * g)
                dve.tensor_tensor(t4[:], mix[:, 4 * g:4 * g + 4, :], rb[:].unsqueeze(1).to_broadcast([P, 4, TOK]),
                                  ALU.mult).then_inc(t4_done, 1)
                dve.wait_ge(t4_done, g + 1)
                for n in range(4):
                    t = 4 * g + n
                    dve.scalar_tensor_tensor(out=mix[:, t, :], in0=t4[:, n, :],
                                             scalar=par[:, t, R_POSTMIX:R_POSTMIX + 1], in1=xr[:, t, :],
                                             op0=ALU.mult, op1=ALU.add).then_inc(x1_done, 1)
                for n in range(4):
                    t = 4 * g + n
                    dve.wait_ge(ahi_done, 3 * NT + t + 1)
                    dve.scalar_tensor_tensor(out=alo[:, t, :], in0=mix[:, t, :],
                                             scalar=par[:, t, R_PREMLP:R_PREMLP + 1],
                                             in1=ahi[:, t, :].bitcast(F32), op0=ALU.mult, op1=ALU.subtract
                                             ).then_inc(act_ready, 1)

            dve.wait_ge(pst_out, 16 * NT)
            rbb = rb2[:].unsqueeze(1).to_broadcast([P, 2, TOK])

            def up(q, i, start=False):
                for c in range(8):
                    ahead(q_up(q), i, c)
                    if start and c == 1:
                        dve.wait_ge(root2, 2)
                        dve.reciprocal(rb2[:], rb2[:]).then_inc(rb2_done, 1)
                        dve.wait_ge(rb2_done, 1)
                    if c % 4 == 3:
                        p = c // 4
                        n = 8 * q + 2 * i + p
                        dve.wait_ge(weights_used, 4 * (q_up(q) + 2 * i + p) + 4)
                        dve.scalar_tensor_tensor(out=rh[:], in0=gemm_bank(p), scalar=0.0, in1=rbb,
                                                 op0=ALU.max, op1=ALU.mult).then_inc(rh_done, 1)
                        dve.wait_ge(hhi_done, n + 1)
                        dve.tensor_tensor(hlo[:, ds(4 * i + 2 * p, 2), :], hs[:],
                                          hhi[:, ds(4 * i + 2 * p, 2), :].bitcast(F32), ALU.subtract
                                          ).then_inc(hid_ready, 1)

            def down(q, i, last=False):
                for c in range(8):
                    if not (last and c >= 6):
                        ahead(q_down(q), i, c)
                    if c % 4 == 3 and not (isinstance(q, int) and q == 0):
                        p = c // 4
                        dve.wait_ge(weights_used, 4 * (q_down(q) + 2 * i + p) + 4)
                        m = ya[:, ds(4 * i + 2 * p, 2), :]
                        dve.tensor_tensor(m, gemm_bank(p), m, ALU.add).then_inc(read_dve, 1)

            up(0, 0, start=True)
            with dve.Fori(1, 4) as i:
                up(0, i)
            with dve.Fori(0, 4) as i:
                down(0, i)
            dve.wait_ge(read_act, 44)
            with dve.Fori(1, 3) as q:
                with dve.Fori(0, 4) as i:
                    up(q, i)
                with dve.Fori(0, 4) as i:
                    down(q, i)
                dve.wait_ge(read_dve, 8 * q + 16)
            with dve.Fori(0, 4) as i:
                up(3, i)
            with dve.Fori(0, 3) as i:
                down(3, i)
            down(3, 3, last=True)

            dve.wait_ge(root2, 3)
            v = st.inc(dve.reciprocal(rb[:], rb[:]))
            dve.wait_ge(dve_step, v)
            dve.wait_ge(read_dve, 40)
            for g in range(4):
                dve.wait_ge(x1_done, NT + 4 * g)
                dve.tensor_tensor(t4[:], ya[:, 4 * g:4 * g + 4, :], rb[:].unsqueeze(1).to_broadcast([P, 4, TOK]),
                                  ALU.mult).then_inc(t4_done, 1)
                dve.wait_ge(t4_done, 4 + g + 1)
                for n in range(4):
                    t = 4 * g + n
                    dve.scalar_tensor_tensor(out=mix[:, t, :], in0=t4[:, n, :],
                                             scalar=par[:, t, R_POSTMLP:R_POSTMLP + 1], in1=mix[:, t, :],
                                             op0=ALU.mult, op1=ALU.add).then_inc(x1_done, 1)

        @block.tensor
        def _(pe):
            def granule(pair, kq, bank, hi, lo, tiles=2):
                pe.wait_ge(lo_done, 4 * pair + kq + 1)
                for n in range(tiles):
                    out = ps[:, bank + n, 0:TOK]
                    for k in range(4):
                        kk = 4 * kq + k
                        wh, wl = whi[:, kq, k, n * P:(n + 1) * P], wlo[:, kq, k, n * P:(n + 1) * P]
                        pe.matmul(out, wh, hi[:, kk, :], start=(kk == 0), stop=False)
                        pe.matmul(out, wh, lo[:, kk, :], start=False, stop=False)
                        last = pe.matmul(out, wl, hi[:, kk, :], start=False, stop=(kk == NT - 1))
                last.then_inc(weights_used, 1)

            pe.wait_ge(consts, 3)
            pe.wait_ge(par_in, 16 * 13)
            for t in range(NT):
                pe.transpose(ps[:, 5 + t // 8, (t % 8) * NROW:(t % 8 + 1) * NROW], prow[:, t * P:(t + 1) * P],
                             ident[0:NROW, 0:NROW])
            for t in range(8):
                last = pe.transpose(ps[:, 6, 360 + 5 * t:365 + 5 * t], prow2[:, t * P:(t + 1) * P],
                                    ident[0:XTAPS + 1, 0:XTAPS + 1])
            last.then_inc(par_trans, 1)
            for c in range(3):
                pe.wait_ge(x_in[c], 16)

            def turn_x(t):
                if t >= 4:
                    pe.wait_ge(x_copied, t - 3)
                    pe.wait_ge(t1_done, t - 3)
                pe.transpose(ps[:, t % 4, 0:P], xn[:, 0, t * P:(t + 1) * P], ident[:])
                pe.transpose(ps[:, t % 4, P:SEQ], xn[:, 1, t * P:(t + 1) * P], ident[:])
                pe.transpose(ps[:, t % 4, SEQ:TOK], xn[0:64, 2, t * P:(t + 1) * P], ident[0:64, 0:64]
                             ).then_inc(x_trans, 1)

            for t in range(4):
                turn_x(t)
            pe.wait_ge(diag_done, 1)
            pe.matmul(ps[:, 4, 0:P], ones[:], diag[:, 0, :], start=True, stop=True)
            pe.matmul(ps[:, 4, P:SEQ], ones[:], diag[:, 1, :], start=True, stop=True)
            pe.matmul(ps[:, 4, SEQ:TOK], ones[:], diag[:, 2, 0:64], start=True, stop=True).then_inc(rb_mm, 1)
            for t in range(4, NT):
                turn_x(t)
            def turn_conv_states(batch):
                pe.wait_ge(par_done, 1)
                pe.wait_ge(cst_in, 32)
                for t in range(4 * batch, 4 * batch + 4):
                    if t >= 2:
                        pe.wait_ge(cst_done, t - 1)
                    for h in range(2):
                        last = pe.transpose(ps[:, 6 + t % 2, h * 120:h * 120 + 120], cst[:, h, t * P:(t + 1) * P],
                                            ident[0:120, 0:120])
                    last.then_inc(cst_trans, 1)

            def turn_xconv_states():
                pe.wait_ge(sst_in, 16)
                pe.wait_ge(cst_done, NT)
                for t in range(NX):
                    last = pe.transpose(ps[:, 7 if t < 12 else 5, (t % 12) * 24:(t % 12) * 24 + 24],
                                        sst[:, t * P:(t + 1) * P], ident[0:24, 0:24])
                last.then_inc(sst_trans, 1)

            pe.wait_ge(rb_done, 1)
            for kq in range(4):
                pe.wait_ge(act_ready, 4 * kq + 4)
                granule(Q_DT, kq, 4, ahi, alo, tiles=1)

            def turn_dt():
                pe.wait_ge(dt_dve, 3)
                for c, off in enumerate((0, P, TOK - P)):
                    last = pe.transpose(ps[:, 4, c * 96:(c + 1) * 96], hst[:, off:off + P], ident[0:96, 0:96])
                last.then_inc(dt_trans, 1)

            def turn_v(i):
                pe.wait_ge(vst_ready, i + 1)
                if isinstance(i, int) and i == 0:
                    pe.wait_ge(sst_done, 1)
                else:
                    pe.wait_ge(vtok_ready, i)
                for n in range(2):
                    last = pe.transpose(ps[0:VNEW, 5, n * P:(n + 1) * P], vst[:, n, :], ident[:])
                last.then_inc(vt_done, 1)

            def glu(i):
                first = isinstance(i, int) and i == 0
                for p in range(2):
                    if first:
                        pe.wait_ge(x_copied, NT)
                    elif p == 0:
                        pe.wait_ge(read_act, i)
                    else:
                        pe.wait_ge(read_dve, i)
                    for kq in range(4):
                        granule(Q_GLU + 2 * i + p, kq, 2 * p, ahi, alo)
                        c = 4 * p + kq
                        if first and 1 <= c <= 4:
                            turn_conv_states(c - 1)
                        if first and c == 5:
                            turn_xconv_states()
                        if first and c == 6:
                            turn_dt()
                        if not first and p == 1 and kq == 0:
                            turn_v(i - 1)

            glu(0)
            with pe.Fori(1, 8) as i:
                glu(i)

            def turn_xw(i):
                pe.wait_ge(xw_ready, 2 * i + 2)
                if isinstance(i, int) and i == 0:
                    pe.wait_ge(vtok_ready, 8)
                else:
                    pe.wait_ge(xtok_ready, i)
                for p in range(2):
                    for n in range(2):
                        last = pe.transpose(ps[0:XNEW, 5, (2 * p + n) * P:(2 * p + n + 1) * P], xw[:, p, n, :],
                                            ident[:])
                last.then_inc(xwt_done, 1)

            def xbc(i):
                first = isinstance(i, int) and i == 0
                for p in range(2):
                    if first:
                        pe.wait_ge(*((read_act, 8) if p == 0 else (read_dve, 8)))
                    else:
                        pe.wait_ge(read_act, 8 + 2 * i + p - 1)
                    for kq in range(4):
                        granule(Q_XBC + 2 * i + p, kq, 2 * p, ahi, alo)
                        if p == 1 and kq == 0:
                            turn_v(7) if first else turn_xw(i - 1)

            xbc(0)
            with pe.Fori(1, 6) as i:
                xbc(i)

            def z(i, tail=False):
                for p in range(2):
                    pe.wait_ge(read_act, 20 + 2 * i + p - 1)
                    for kq in range(4):
                        granule(Q_Z + 2 * i + p, kq, 2 * p, ahi, alo)
                        if isinstance(i, int) and i == 0 and p == 1 and kq == 0:
                            turn_xw(5)
                        if tail and p == 0 and kq == 0:
                            pe.wait_ge(msum_done, 1)
                            pe.wait_ge(dt_ready, 1)
                            pe.matmul(ps[:, 4, 0:TOK], ones[:], msum[:], start=True, stop=True
                                      ).then_inc(mean_mm, 1)
                        if tail and p == 1:
                            pe.wait_ge(sq_ready, kq + 1)
                            if kq == 0:
                                pe.wait_ge(mean_done, 1)
                            for n in range(4):
                                last = pe.matmul(ps[:, 4, 0:TOK], ones[:], sqb[:, n, :],
                                                 start=(kq == 0 and n == 0), stop=(kq == 3 and n == 3))
                            last.then_inc(sq_used, 1)

            z(0)
            with pe.Fori(1, 3) as i:
                z(i)
            z(3, tail=True)

            def scan_front(i, j):
                T = 4 * i + j
                first = isinstance(i, int) and i == 0 and j == 0
                if j == 0:
                    pe.wait_ge(bt_ready, i + 1)
                    if not first:
                        pe.wait_ge(pst_done, T)
                        pe.wait_ge(hts_ready, T)
                        pe.wait_ge(mixw_done, 2 * T)
                    else:
                        pe.wait_ge(var_root, 1)
                        pe.wait_ge(read_act, 28)
                    for c, off in enumerate((0, P, TOK - P)):
                        last = pe.transpose(ps[:, 4, c * P:(c + 1) * P], bt[:, off:off + P], ident[:])
                    last.then_inc(bt_trans, 1)
                    for c, off in enumerate((0, P, TOK - P)):
                        hi = min((c + 1) * P, TOK)
                        last = pe.matmul(ps[:, 2, c * P:hi], bt[:, off:off + P], xb[:, NT + GROUPS + i, c * P:hi],
                                         start=True, stop=True)
                    last.then_inc(cb_done, 1)
                    pe.wait_ge(btok_ready, i + 1)
                else:
                    pe.wait_ge(pst_done, T)
                pe.wait_ge(xst_ready, T + 1)
                for c, off in enumerate((0, P, TOK - P)):
                    last = pe.transpose(ps[:, 4, c * P:(c + 1) * P], xst[:, off:off + P], ident[:])
                last.then_inc(xtile_trans, 1)
                segment(T, 0, first)
                pe.wait_ge(h0_in[j % 2], 16 * (2 * i + j // 2 + 1))
                if not first:
                    pe.wait_ge(hnew_done, T)
                for b in range(NB):
                    last = pe.transpose(ps[:, 6 + b // 4, (b % 4) * P:(b % 4 + 1) * P], h0[:, j % 2, b, :],
                                        ident[:])
                last.then_inc(h0_trans, 1)
                pe.wait_ge(xd_ready, T + 1)
                pe.wait_ge(btok_ready, i + 1)
                pe.matmul(ps[:, 4, 384:512], btok[:, 0, :], xdd[:, 0, :], start=True, stop=True
                          ).then_inc(pstart_done, 1)

            def segment(T, e, first):
                if not (first and e == 0):
                    pe.wait_ge(exp_done, 2 * T + e)
                seg = ps[:, 3, 0:TOK]
                pe.matmul(seg, identb[:], mneg[:], start=True, stop=False)
                pe.matmul(seg, sel[:, ds(2 * T + e, 1)].to_broadcast([P, P]), cum3[:], start=False, stop=False)
                for c, off in enumerate((0, P, TOK - P)):
                    lo, hi = c * P, min((c + 1) * P, TOK)
                    last = pe.matmul(ps[:, 3, lo:hi], cum3[:, off:off + P],
                                     nsel[:, ds(2 * T + e, 1)].to_broadcast([P, hi - lo]), start=False, stop=(c == 2))
                last.then_inc(seg_done, 1)

            def within(T, e):
                for c in range(3):
                    lo, hi = c * P, min((c + 1) * P, TOK)
                    last = pe.matmul(ps[e * HD:(e + 1) * HD, 5, lo:hi], xd[:, c, e * HD:(e + 1) * HD],
                                     wgt[:, e, lo:hi], start=True, stop=True)
                return last

            def scan_back(i, j):
                T = 4 * i + j
                first = isinstance(i, int) and i == 0 and j == 0
                segment(T, 1, first)
                if not first:
                    pe.wait_ge(ecb_ready, T)
                pe.wait_ge(selt_ready, T + 1)
                pe.wait_ge(mixw_done, 2 * T + 1)
                pe.matmul(ps[:, 2, TOK:512], selt[:].rearrange("p h d -> p (h d)"),
                          ecum3[:, P:TOK], start=True, stop=True).then_inc(ecb_mm, 1)
                if not first:
                    pe.wait_ge(y_read, T)
                within(T, 0)
                pe.wait_ge(h0t_ready, T + 1)
                for b in range(NB):
                    pe.matmul(ps[:, 5, 448 + DS * b:456 + DS * b], h0t[:, b, :],
                              xb[:, NT + GROUPS + i, SEQ + DS * b:SEQ + DS * (b + 1)], start=True, stop=True)
                pe.wait_ge(hts_ready, T + 1)
                pe.matmul(ps[:, 5, TOK:448], hts[:], xb[:, NT + GROUPS + i, P:SEQ], start=True, stop=True)
                for c in range(2):
                    pe.matmul(ps[:, 4, c * P:(c + 1) * P], xdd[:, c, :], btok[:, c, :], start=True, stop=True)
                pe.wait_ge(bm_ready, i + 1)
                for h in range(2):
                    last = pe.matmul(ps[:, 6 + h, :], xdd[:, 2, :], bm[:, 4 * h:4 * h + 4, :], start=True, stop=True)
                last.then_inc(st_done, 1)
                pe.wait_ge(mixw_done, 2 * T + 2)
                within(T, 1).then_inc(y_done, 1)

            def wc(i):
                first = isinstance(i, int) and i == 0
                for j in range(4):
                    p, kq = j // 2, 2 * (j % 2)
                    if first and j < 2:
                        pe.wait_ge(act_ready, NT + 4 * kq + 4)
                    if kq == 0:
                        pe.wait_ge(read_act, 28 + 2 * i + p)
                    granule(Q_WC + 2 * i + p, kq, 0, ahi, alo)
                    scan_front(i, j)
                    if first and j < 2:
                        pe.wait_ge(act_ready, NT + 4 * kq + 8)
                    granule(Q_WC + 2 * i + p, kq + 1, 0, ahi, alo)
                    scan_back(i, j)

            wc(0)
            with pe.Fori(1, 4) as i:
                wc(i)

            pe.wait_ge(gss_done, 1)
            pe.wait_ge(y_read, NT)
            pe.wait_ge(pst_done, NT)
            pe.wait_ge(mixw_done, 2 * NT)
            for g in range(GROUPS):
                last = pe.matmul(ps[:, 2 + g, 0:TOK], ones[:], gss[:, g, :], start=True, stop=True)
            last.then_inc(gn_mm, 1)

            def gemm(pair0, i, hi, lo, counts, operand=None):
                for p in range(2):
                    for s, v in counts(p):
                        pe.wait_ge(s, v)
                    for kq in range(4):
                        if operand and p == 0:
                            pe.wait_ge(operand[0], operand[1] + operand[2] * (kq + 1))
                        granule(pair0 + 2 * i + p, kq, 2 * p, hi, lo)

            gemm(Q_WS, 0, ahi, alo, lambda p: [(read_act, 36), (gn_root, 1)], (act_ready, 2 * NT, 4))
            with pe.Fori(1, 4) as i:
                gemm(Q_WS, i, ahi, alo, lambda p: [(read_dve, 8 + 2 * i + p - 1)])

            pe.wait_ge(acc_done, 1)
            for n in range(2):
                last = pe.matmul(ps[:, 4, 0:TOK], ones[:], acc2[:, n, :], start=(n == 0), stop=(n == 1))
            last.then_inc(rms_mm, 1)

            def rms_x1():
                pe.wait_ge(acc_done, 2)
                for n in range(2):
                    last = pe.matmul(ps[:, 5, 0:TOK], ones[:], acc2[:, n, :], start=(n == 0), stop=(n == 1))
                last.then_inc(rms_mm, 1)

            def up0(q, counts):
                gemm(q_up(q), 0, ahi, alo, counts)

            for p in range(2):
                pe.wait_ge(read_dve, 15 + p)
                for kq in range(4):
                    if p == 0:
                        pe.wait_ge(act_ready, 3 * NT + 4 * (kq + 1))
                    granule(q_up(0) + p, kq, 2 * p, ahi, alo)
                    if p == 0 and kq == 0:
                        rms_x1()
            with pe.Fori(1, 4) as i:
                gemm(q_up(0), i, ahi, alo, lambda p: [(rh_done, 2 * i + p - 1)])
            gemm(q_down(0), 0, hhi, hlo, lambda p: [(rh_done, 7 + p)], (hid_ready, 0, 2))
            with pe.Fori(1, 4) as i:
                gemm(q_down(0), i, hhi, hlo, lambda p: [(read_act, 36 + 2 * i + p - 1)])

            def quarter(q, last_read):
                gemm(q_up(q), 0, ahi, alo, last_read)
                with pe.Fori(1, 4) as i:
                    gemm(q_up(q), i, ahi, alo, lambda p: [(rh_done, 8 * q + 2 * i + p - 1)])
                gemm(q_down(q), 0, hhi, hlo, lambda p: [(rh_done, 8 * q + 7 + p)], (hid_ready, 8 * q, 2))
                with pe.Fori(1, 4) as i:
                    gemm(q_down(q), i, hhi, hlo, lambda p: [(read_dve, 8 + 8 * q + 2 * i + p - 1)])

            quarter(1, lambda p: [(read_act, 43 + p)])
            with pe.Fori(2, 4) as q:
                quarter(q, lambda p: [(read_dve, 8 + 8 * q - 1 + p)])

            pe.wait_ge(acc_done, 3)
            for n in range(2):
                last = pe.matmul(ps[:, 4, 0:TOK], ones[:], acc2[:, n, :], start=(n == 0), stop=(n == 1))
            last.then_inc(rms_mm, 1)
            pe.wait_ge(root2, 3)
            for g in range(4):
                pe.wait_ge(x1_done, NT + 4 * g + 4)
                if g >= 2:
                    pe.wait_ge(ot_copied, g - 1)
                b = 3 * (g % 2)
                for n in range(4):
                    t, cols = 4 * g + n, slice(n * P, (n + 1) * P)
                    pe.transpose(ps[:, b, cols], mix[:, t, 0:P], ident[:])
                    pe.transpose(ps[:, b + 1, cols], mix[:, t, P:SEQ], ident[:])
                    last = pe.transpose(ps[0:64, b + 2, cols], mix[:, t, SEQ:TOK], ident[:])
                last.then_inc(ot_trans, 1)


_INS = ["x_prompt", "x_sample", "state_ssm", "state_ssd_conv", "state_conformer_conv", "w_in", "ssd_conv_w",
        "ssd_conv_b", "dt_bias", "a_log", "d_skip", "ssd_norm_w", "conf_conv_w", "conf_conv_b", "conf_norm_w",
        "conf_norm_b", "w_out", "norm_pre_mix", "norm_post_mix", "norm_pre_mlp", "norm_post_mlp", "w_up",
        "w_down"]
_OUTS = [(1, SEQ, D), (NB, DS, D), (1, 1, HEADS, HD, STATE), (1, 1, XHALO, D_XBC), (1, 1, HALO, D),
         (1, NB, HEADS, HD, STATE), (1, NB, XHALO, D_XBC), (1, NB, HALO, D)]


def kernel(**inputs):
    import concourse.bacc as bacc
    from concourse.bass_utils import run_bass_kernel_spmd as run

    nc = bacc.Bacc("TRN2", target_bir_lowering=False, num_devices=1)
    arrays, args = {}, []
    for name in _INS:
        a = np.ascontiguousarray(inputs[name])
        arrays[f"in_{name}"] = a
        args.append(nc.dram_tensor(f"in_{name}", a.shape, mybir.dt.from_np(a.dtype), kind="ExternalInput").ap())
    for i, shape in enumerate(_OUTS):
        args.append(nc.dram_tensor(f"out_{i}", shape, F32, kind="ExternalOutput").ap())
    args.append(nc.dram_tensor("x_transposed", (P, NT * TOK), F32, kind="Internal").ap())
    build(nc, *args)
    r = run(nc, [arrays], core_ids=[0])
    return tuple(r.results[0][f"out_{i}"] for i in range(len(_OUTS)))
```

```python
from contextlib import ExitStack

import numpy as np

import concourse.bass as bass
from concourse import mybir

F32 = mybir.dt.float32
F32R = mybir.dt.float32r
BF16 = mybir.dt.bfloat16
ALU = mybir.AluOpType
ACT = mybir.ActivationFunctionType
ds = bass.ds

P = 128
D = 2048
NT = D // P
SEQ = 256
NB, DS = 8, 8
TOK = SEQ + NB * DS
HEADS, HD, GROUPS, STATE = 32, 64, 4, 128
D_XBC = D + 2 * GROUPS * STATE
NX = D_XBC // P
TAPS, XTAPS = 31, 4
HALO, XHALO = TAPS - 1, XTAPS - 1
D_FF = 4 * D
COL_Z, COL_XBC, COL_DT, COL_GLU = 0, D, D + D_XBC, D + D_XBC + HEADS
EPS = 1e-6
MASKED = -1.0e30

PEXT = HALO + SEQ
SEXT = HALO + DS
VLEN = PEXT + NB * SEXT
XPEXT = XHALO + SEQ
XSEXT = XHALO + DS
XLEN = XPEXT + NB * XSEXT
VNEW = HALO + NB * DS
XNEW = XHALO + NB * XHALO

R_CONV, R_CB, R_NW, R_NB, R_SSD, R_PREMIX, R_POSTMIX, R_PREMLP, R_POSTMLP, R_XW, R_XB, R_DSKIP = (
    1, 32, 33, 34, 35, 36, 37, 38, 39, 40, 44, 0)
NROW = 45

Q_DT, Q_GLU, Q_XBC, Q_Z, Q_WC, Q_WS, Q_MLP = 0, 1, 17, 29, 37, 45, 53
Q_END = Q_MLP + 4 * 16


def q_up(q):
    return Q_MLP + 16 * q


def q_down(q):
    return Q_MLP + 16 * q + 8


class Steps:

    def __init__(self, sem):
        self.sem, self.at, self.made = sem, 0, 0

    def inc(self, ins):
        ins.then_inc(self.sem, 1)
        self.at = self.at + 1
        self.made += 1
        return self.at

    def enter(self, i, first, per):
        self.top, self.per, self.first = self.at, per, first
        self.at = (i - first) * per + self.top
        self.made = 0

    def leave(self, turns):
        assert self.made == self.per, (self.made, self.per)
        self.at = self.top + turns * self.per


def build(nc, x_prompt, x_sample, state_ssm, state_ssd_conv, state_conf, w_in, ssd_conv_w, ssd_conv_b,
          dt_bias, a_log, d_skip, ssd_norm_w, conf_conv_w, conf_conv_b, conf_norm_w, conf_norm_b, w_out,
          norm_pre_mix, norm_post_mix, norm_pre_mlp, norm_post_mlp, w_up, w_down,
          y_prompt, y_sample, p_ssm, p_sc, p_cc, s_ssm, s_sc, s_cc, xt_dram):
    with ExitStack() as ctx:
        def sem(name):
            return ctx.enter_context(nc.semaphore(name))

        slab = ctx.enter_context(nc.sbuf_tensor("slab", [P, 53200], F32, align_bytes=64))
        base = (int(nc.sbuf_base) - 53200 * 4)
        cursor = [0]

        def place(name, shape, dt=F32, at=None):
            size = int(np.prod(shape[1:])) * (2 if dt == BF16 else 4)
            size = -(-size // 32) * 8
            off = cursor[0] if at is None else at
            if at is None:
                cursor[0] += size
            assert off + size <= 53200, (name, off, size)
            return nc.alloc_sbuf_tensor_at(name, shape, dt, offset=base + 4 * off)

        a_off = 0
        ahi = place("ahi", [P, NT, TOK], F32R)
        alo = place("alo", [P, NT, TOK], F32R)
        raw = place("raw", [P, 4, 4, 256])
        whi = place("whi", [P, 4, 4, 256], F32R)
        wlo = place("wlo", [P, 4, 4, 256], F32R)
        ar = cursor[0]
        cursor[0] += 22240
        vx = place("vx", [P, NT, VLEN], at=ar)
        xb = place("xb", [P, NX, TOK], at=ar + NT * VLEN)
        zg = place("zg", [P, NT, TOK], at=ar + NT * VLEN + NX * TOK)
        xn = place("xn", [P, 3, D], at=ar)
        xt0 = place("xt0", [P, NT, TOK], at=ar + 6144)
        cst = place("cst", [4 * HALO, 2, D], at=ar + 11264)
        sst = place("sst", [NB * XHALO, D_XBC], at=ar + 15360)
        prow = place("prow", [NROW, D], at=ar + 18432)
        prow2 = place("prow2", [XTAPS + 1, D_XBC - D], at=ar + 20480)
        mix = place("mix", [P, NT, TOK], at=ar)
        sc = ar + 5120
        bt = place("bt", [P, TOK], at=sc)
        xst = place("xst", [P, TOK], at=sc + 320)
        btok = place("btok", [P, 3, P], at=sc + 640)
        bm = place("bm", [P, NB, P], at=sc + 1024)
        xd = place("xd", [P, 3, P], at=sc + 2048)
        xdd = place("xdd", [P, 3, P], at=sc + 2432)
        h0t = place("h0t", [P, NB, P], at=sc + 2816)
        pst = place("pst", [P, P], at=sc + 3840)
        s0s = place("s0s", [P, P], at=sc + 3968)
        yoff = place("yoff", [P, 192], at=sc + 4096)
        xr = place("xr", [P, NT, TOK], at=ar + NT * VLEN)
        hhi = place("hhi", [P, NT, TOK], F32R, at=ar + 5120)
        hlo = place("hlo", [P, NT, TOK], F32R, at=ar + 10240)
        ya = place("ya", [P, NT, TOK], at=ar + 15360)
        yo = place("yo", [P, 3, D], at=a_off)
        par = place("par", [P, NT, NROW])
        sw = place("sw", [P, NX, XTAPS + 1])
        ident = place("ident", [P, P])
        identb = place("identb", [P, P], BF16)
        ones = place("ones", [P, P])
        mean1 = place("mean1", [P, P])
        mneg = place("mneg", [P, TOK], BF16)
        sel = place("sel", [P, HEADS], BF16)
        nsel = place("nsel", [P, HEADS], BF16)
        cum3 = place("cum3", [P, TOK], BF16)
        ecum3 = place("ecum3", [P, TOK], BF16)
        tcol = place("tcol", [P, 3, 96])
        blk = place("blk", [P, NB])
        eps = place("eps", [P, 2])
        sqp = place("sqp", [P, TOK], at=cursor[0])
        rb = place("rb", [P, TOK])
        dcol = place("dcol", [HEADS, 2])
        selt = place("selt", [P, 2, HD], BF16)
        sm = cursor[0]
        xs = place("xs", [P, NX, NB * XHALO])
        xe = place("xe", [P, 2, 2, XLEN])
        vst = place("vst", [P, 2, VNEW])
        vtok = place("vtok", [VNEW, 256])
        xw = place("xw", [P, 2, 2, XNEW])
        xtok = place("xtok", [XNEW, 512])
        vacc = place("vacc", [P, 2, TOK])
        sqs = place("sqs", [P, TOK], at=cursor[0])
        sg = place("sg", [P, 2, TOK])
        msum = place("msum", [P, TOK])
        own = cursor[0]
        sqb = place("sqb", [P, 4, TOK])
        t1 = place("t1", [P, 2, TOK], at=own)
        ss = place("ss", [P, 4], at=own + 640)
        diag = place("diag", [P, 3, P], at=own + 648)
        dsk = place("dsk", [1, HEADS], at=sm)
        hw = place("hw", [HEADS, 8, TOK], at=ar + 18432)
        hst = place("hst", [96, TOK], at=ar + 18432 + 8 * TOK)
        hb = place("hb", [HEADS, 3, TOK], BF16, at=ar + 18432 + 9 * TOK)
        wgt = place("wgt", [P, 2, TOK], at=sm)
        h0 = place("h0", [P, 2, NB, P], at=sm + 640)
        hout = place("hout", [P, NB, P], at=sm + 2688)
        ecb = place("ecb", [P, 192], at=sm + 3712)
        hts = place("hts", [P, P], at=sm + 3904)
        ysum = place("ysum", [P, TOK], at=sm + 4032)
        gss = place("gss", [P, GROUPS, TOK], at=sm + 4352)
        sq2 = place("sq2", [P, 2, TOK], at=sm)
        acc2 = place("acc2", [P, 2, TOK], at=sm + 640)
        rh = place("rh", [P, 2, TOK], at=sm + 1280)
        hs = place("hs", [P, 2, TOK], at=sm + 1920)
        t4 = place("t4", [P, 4, TOK], at=sm + 2560)
        rb2 = place("rb2", [P, TOK], at=sm + 3840)
        ps = ctx.enter_context(nc.psum_tensor("ps", [P, 8, 512], F32))

        raw_ready = [sem(f"raw_ready{s}") for s in range(4)]
        hi_done, weights_used = sem("hi_done"), sem("weights_used")
        lo_done = [sem(f"lo_done{s}") for s in range(4)]
        ahi_done, act_ready = sem("ahi_done"), sem("act_ready")
        read_act, read_dve = sem("read_act"), sem("read_dve")
        pool_turn, act_turn = sem("pool_turn"), sem("act_turn")
        dve_step, pool_step = sem("dve_step"), sem("pool_step")
        x_in = [sem(f"x_in{c}") for c in range(3)]
        dsk_in, dsk_done = sem("dsk_in"), sem("dsk_done")
        par_in, cst_in, sst_in, dcol_in = sem("par_in"), sem("cst_in"), sem("sst_in"), sem("dcol_in")
        consts = sem("consts")
        x_trans, x_copied, t1_done = sem("x_trans"), sem("x_copied"), sem("t1_done")
        par_trans, par_copied, par_done = sem("par_trans"), sem("par_copied"), sem("par_done")
        rooted = sem("rooted")
        ss_done, diag_done, rb_mm, rb_done = sem("ss_done"), sem("diag_done"), sem("rb_mm"), sem("rb_done")
        cst_trans, cst_done, sst_trans, sst_done = (
            sem("cst_trans"), sem("cst_done"), sem("sst_trans"), sem("sst_done"))
        xt_stored, halo_zero = sem("xt_stored"), sem("halo_zero")
        dt_act, dt_dve, dt_trans, dt_ready = sem("dt_act"), sem("dt_dve"), sem("dt_trans"), sem("dt_ready")
        vst_ready, vt_done, vtok_ready, vout = (
            sem("vst_ready"), sem("vt_done"), sem("vtok_ready"), sem("vout"))
        conv_turn, conv_begun, msum_done = sem("conv_turn"), sem("conv_begun"), sem("msum_done")
        xconv_done, xb_done, xw_ready, xwt_done, xtok_ready, xout = (
            sem("xconv_done"), sem("xb_done"), sem("xw_ready"), sem("xwt_done"), sem("xtok_ready"), sem("xout"))
        mean_mm, mean_done, cent_done, sq_ready, sq_summed, sq_used, var_root, cn_done, silu_done = (
            sem("mean_mm"), sem("mean_done"), sem("cent_done"), sem("sq_ready"), sem("sq_summed"), sem("sq_used"),
            sem("var_root"), sem("cn_done"), sem("silu_done"))
        bt_ready, bt_trans, btok_ready, bm_ready, cb_done = (
            sem("bt_ready"), sem("bt_trans"), sem("btok_ready"), sem("bm_ready"), sem("cb_done"))
        xst_ready, xtile_trans, xd_ready, seg_done, exp_done, mixw_done = (
            sem("xst_ready"), sem("xtile_trans"), sem("xd_ready"), sem("seg_done"), sem("exp_done"),
            sem("mixw_done"))
        h0_in = [sem("h0_in0"), sem("h0_in1")]
        h0_trans, h0t_ready, pstart_done, hts_ready = (
            sem("h0_trans"), sem("h0t_ready"), sem("pstart_done"), sem("hts_ready"))
        selt_ready = sem("selt_ready")
        ecb_mm, ecb_ready, st_done, hnew_done, pst_done, y_done, y_read, g_done = (
            sem("ecb_mm"), sem("ecb_ready"), sem("st_done"), sem("hnew_done"), sem("pst_done"),
            sem("y_done"), sem("y_read"), sem("g_done"))
        hout_out, pst_out = sem("hout_out"), sem("pst_out")
        gss_done, gn_mm, gn_root, gn_done = sem("gss_done"), sem("gn_mm"), sem("gn_root"), sem("gn_done")
        xr_in, acc_done, rms_mm, rms_done, t4_done, x1_done = (
            sem("xr_in"), sem("acc_done"), sem("rms_mm"), sem("rms_done"), sem("t4_done"),
            sem("x1_done"))
        rh_done, hs_done, hhi_done, hid_ready = sem("rh_done"), sem("hs_done"), sem("hhi_done"), sem("hid_ready")
        ot_trans, ot_copied, y_out, old_rows = sem("ot_trans"), sem("ot_copied"), sem("y_out"), sem("old_rows")

        def rows(w, r0):
            return w[ds(r0, D), :].rearrange("(k p) n -> p k n", p=P)

        w_in2, w_out2, w_up2, w_down2 = w_in[0], w_out[0], w_up[0], w_down[0]
        in_k, ssd_k, conf_k, up_k = rows(w_in2, 0), rows(w_out2, 0), rows(w_out2, D), rows(w_up2, 0)
        down_k = w_down2.rearrange("(q k p) n -> p q k n", p=P, k=NT)

        def v_prompt(t, n, lo, hi):
            return vx[:, ds(t, n), lo:hi]

        def v_sample(t, n, lo, hi):
            return vx[:, ds(t, n), PEXT:VLEN].rearrange("p n (b j) -> p n b j", b=NB)[:, :, :, lo:hi]

        def v_sample1(t, lo, hi):
            return vx[:, t, PEXT:VLEN].rearrange("p (b j) -> p b j", b=NB)[:, :, lo:hi]

        def seqs(ap):
            return ap.rearrange("p (b j) -> p b j", b=NB)

        def gemm_bank(p):
            return ps[:, 2 * p:2 * p + 2, 0:TOK]

        block = ctx.enter_context(nc.Block())

        @block.sync
        def _(sp):
            for c in range(2):
                sp.dma_start(xn[:, c, :], x_prompt[0, c * P:(c + 1) * P, :]).then_inc(x_in[c], 16)
            sp.dma_start(xn[0:NB * DS, 2, :], x_sample.rearrange("b s d -> (b s) d")).then_inc(x_in[2], 16)

            def load(src, pair, kq, width=256):
                if not (isinstance(pair, int) and pair == 0):
                    sp.wait_ge(lo_done[kq], pair)
                sp.dma_start(raw[:, kq, :, 0:width], src).then_inc(raw_ready[kq], 16)

            for kq in range(4):
                load(in_k[:, 4 * kq:4 * kq + 4, COL_DT:COL_DT + P], Q_DT, kq, P)

            def body(mat, pair0, cols, i):
                for p in range(2):
                    for kq in range(4):
                        load(mat[:, 4 * kq:4 * kq + 4, ds(cols[p] , 256)], pair0 + 2 * i + p, kq)

            with sp.Fori(0, 8) as i:
                body(in_k, Q_GLU, (COL_GLU + D + 256 * i, COL_GLU + 256 * i), i)
            with sp.Fori(0, 6) as i:
                body(in_k, Q_XBC, (COL_XBC + 512 * i, COL_XBC + 512 * i + 256), i)
            with sp.Fori(0, 4) as i:
                body(in_k, Q_Z, (COL_Z + 512 * i, COL_Z + 512 * i + 256), i)
            with sp.Fori(0, 4) as i:
                body(conf_k, Q_WC, (512 * i, 512 * i + 256), i)
            with sp.Fori(0, 4) as i:
                body(ssd_k, Q_WS, (512 * i, 512 * i + 256), i)
            with sp.Fori(0, 4) as q:
                with sp.Fori(0, 4) as i:
                    body(up_k, q_up(q), (D * q + 512 * i, D * q + 512 * i + 256), i)
                with sp.Fori(0, 4) as i:
                    for p in range(2):
                        for kq in range(4):
                            load(down_k[:, q, 4 * kq:4 * kq + 4, ds(512 * i + 256 * p, 256)],
                                 q_down(q) + 2 * i + p, kq)

        @block.gpsimd
        def _(pool):
            st = Steps(pool_step)
            pool.memset(ident[:], 0.0)
            pool.memset(identb[:], 0.0)
            pool.memset(ones[:], 1.0)
            pool.memset(eps[:], EPS)
            pool.memset(mean1[:], 1.0 / D)
            pool.memset(mneg[:], 0.0)
            pool.memset(sel[:], 0.0)
            pool.memset(nsel[:], 0.0)
            pool.memset(ss[:], 1.0)
            pool.memset(cum3[:], 0.0)
            pool.memset(ecum3[:], 0.0)
            v = st.inc(pool.memset(blk[:], 1.0))
            pool.wait_ge(pool_step, v)
            for m in (ident, identb):
                pool.affine_select(out=m[:], in_=m[:], compare_op=ALU.not_equal, fill=1.0, base=0,
                                   pattern=[[-1, P]], channel_multiplier=1).then_inc(consts, 1)
            for c in range(2):
                half = mneg[:, c * P:(c + 1) * P]
                pool.affine_select(out=half, in_=half, compare_op=ALU.is_ge, fill=MASKED, base=0,
                                   pattern=[[1, P]], channel_multiplier=-1)
            third = seqs(mneg[:, SEQ:TOK])
            v = st.inc(pool.affine_select(out=third, in_=third, compare_op=ALU.is_ge, fill=MASKED, base=64,
                                          pattern=[[DS, NB], [1, DS]], channel_multiplier=-1))
            pool.wait_ge(pool_step, v)
            pool.affine_select(out=third, in_=third, compare_op=ALU.is_ge, fill=MASKED, base=-64,
                               pattern=[[-DS, NB], [0, DS]], channel_multiplier=1)
            for m, one in ((sel, 1.0), (nsel, -1.0)):
                for part in range(3):
                    v = st.inc(pool.affine_select(out=m[:], in_=m[:], compare_op=ALU.not_equal, fill=one,
                                                  base=-HEADS * part, pattern=[[-1, HEADS]],
                                                  channel_multiplier=1))
                    pool.wait_ge(pool_step, v)
            v = st.inc(pool.affine_select(out=blk[:], in_=blk[:], compare_op=ALU.is_ge, fill=0.0, base=-64,
                                          pattern=[[-DS, NB]], channel_multiplier=1))
            pool.wait_ge(pool_step, v)
            pool.affine_select(out=blk[:], in_=blk[:], compare_op=ALU.is_ge, fill=0.0, base=64 + DS - 1,
                               pattern=[[DS, NB]], channel_multiplier=-1).then_inc(consts, 1)

            for h in range(2):
                pool.dma_start(cst[:, h, :], state_conf[0, 4 * h:4 * h + 4].rearrange("b j d -> (b j) d")
                               ).then_inc(cst_in, 16)
            pool.dma_start(sst[:], state_ssd_conv[0].rearrange("b j d -> (b j) d")).then_inc(sst_in, 16)
            pool.dma_start(dcol[:, 0:1], dt_bias.rearrange("o h -> h o")).then_inc(dcol_in, 16)
            pool.dma_start(dcol[:, 1:2], a_log.rearrange("o h -> h o")).then_inc(dcol_in, 16)
            pool.dma_start(s_cc[0, :, 0:HALO - DS, :], state_conf[0, :, DS:HALO, :]).then_inc(old_rows, 16)

            pool.memset(xe[:, :, :, 0:XHALO], 0.0)
            pool.memset(msum[:], 0.0)
            pool.wait_ge(x_trans, NT)
            pool.wait_ge(xt_stored, 16)
            pool.memset(vx[:, :, 0:HALO], 0.0).then_inc(halo_zero, 1)

            def plain():
                pool.sem_inc(pool_turn, 1)

            def gather_v(i):
                pool.wait_ge(read_dve, i + 1)
                if not (isinstance(i, int) and i == 0):
                    pool.wait_ge(vt_done, i)
                plain()
                pool.tensor_copy(vst[:, :, 0:HALO], v_prompt(2 * i, 2, SEQ, PEXT))
                for n in range(2):
                    last = pool.tensor_copy(seqs(vst[:, n, HALO:VNEW]), v_sample1(2 * i + n, HALO, SEXT))
                last.then_inc(vst_ready, 1)

            def store_v(i):
                pool.wait_ge(vtok_ready, i + 1)
                pool.dma_start(p_cc[0, 0, :, ds(256 * i, 256)], vtok[0:HALO, :]).then_inc(vout, 16)
                pool.dma_start(s_cc[0, :, HALO - DS:HALO, ds(256 * i, 256)], vtok[HALO:VNEW, :]
                               ).then_inc(vout, 16)

            def sum_tile(j):
                pool.wait_ge(conv_turn, j + 2)
                pool.wait_ge(pool_step, st.at)
                plain()
                pool.tensor_tensor(msum[:, 0:SEQ], msum[:, 0:SEQ], vx[:, j, 0:SEQ], ALU.add)
                st.inc(pool.tensor_tensor(seqs(msum[:, SEQ:TOK]), seqs(msum[:, SEQ:TOK]),
                                          v_sample1(j, 0, DS), ALU.add))

            def split(pair0, i, c):
                pair, kq = pair0 + 2 * i + (c + 2) // 4, (c + 2) % 4
                pool.wait_ge(hi_done, 4 * pair + kq + 1)
                pool.tensor_tensor(wlo[:, kq, :, :], raw[:, kq, :, :], whi[:, kq, :, :].bitcast(F32),
                                   ALU.subtract).then_inc(lo_done[kq], 1)

            def glu(i):
                first = isinstance(i, int) and i == 0
                split(Q_GLU, i, 1)
                split(Q_GLU, i, 3)
                split(Q_GLU, i, 5)
                if not first:
                    store_v(i - 1)
                split(Q_GLU, i, 7)
                gather_v(i)
                if not first:
                    sum_tile(i - 1)

            glu(0)
            with pool.Fori(1, 8) as i:
                st.enter(i, 1, 1)
                glu(i)
                st.leave(7)

            def gather_x(i, p):
                pool.wait_ge(read_act, 8 + 2 * i + p + 1)
                if p == 0 and not (isinstance(i, int) and i == 0):
                    pool.wait_ge(xwt_done, i)
                plain()
                pool.tensor_copy(xw[:, p, :, 0:XHALO], xe[:, p, :, XPEXT - XHALO:XPEXT])
                for n in range(2):
                    last = pool.tensor_copy(
                        seqs(xw[:, p, n, XHALO:XNEW]), seqs(xe[:, p, n, XPEXT:XLEN])[:, :, XSEXT - XHALO:XSEXT])
                last.then_inc(xw_ready, 1)

            def store_x(i):
                pool.wait_ge(xtok_ready, i + 1)
                pool.dma_start(p_sc[0, 0, :, ds(512 * i, 512)], xtok[0:XHALO, :]).then_inc(xout, 16)
                pool.dma_start(s_sc[0].rearrange("b j d -> (b j) d")[:, ds(512 * i, 512)], xtok[XHALO:XNEW, :]
                               ).then_inc(xout, 16)

            def xbc(i):
                split(Q_XBC, i, 1)
                split(Q_XBC, i, 3)
                gather_x(i, 0)
                split(Q_XBC, i, 5)
                if isinstance(i, int) and i == 0:
                    store_v(7)
                else:
                    store_x(i - 1)
                split(Q_XBC, i, 7)
                gather_x(i, 1)
                sum_tile(7 + i)

            xbc(0)
            with pool.Fori(1, 6) as i:
                st.enter(i, 1, 1)
                xbc(i)
                st.leave(5)

            def z(i):
                for c in (1, 3, 5):
                    split(Q_Z, i, c)
                if isinstance(i, int) and i == 0:
                    store_x(5)
                split(Q_Z, i, 7)
                sum_tile(13 + i)

            z(0)
            with pool.Fori(1, 3) as i:
                st.enter(i, 1, 1)
                z(i)
                st.leave(2)
            pool.wait_ge(pool_step, st.at)
            pool.sem_inc(msum_done, 1)
            for c in (1, 3, 5, 7):
                split(Q_Z, 3, c)

            def square_tile(i, j):
                pool.wait_ge(g_done, 4 * i + j + 1)
                plain()
                g = zg[:, 4 * i + j, :]
                if j == 0:
                    st.inc(pool.tensor_tensor(gss[:, i, :], g, g, ALU.mult))
                    return
                v = st.inc(pool.tensor_tensor(sqp[:], g, g, ALU.mult))
                pool.wait_ge(pool_step, v)
                plain()
                st.inc(pool.tensor_tensor(gss[:, i, :], gss[:, i, :], sqp[:], ALU.add))
                pool.wait_ge(pool_step, st.at)
                plain()

            pool.wait_ge(act_ready, 2 * NT)
            with pool.Fori(0, 4) as i:
                st.enter(i, 0, 7)
                for j in range(4):
                    pool.tensor_copy(selt[:], sel[:, ds(8 * i + 2 * j, 2)].unsqueeze(2).to_broadcast([P, 2, HD])
                                     ).then_inc(selt_ready, 1)
                    square_tile(i, j)
                st.leave(4)
            pool.wait_ge(pool_step, st.at)
            pool.sem_inc(gss_done, 1)
            pool.wait_ge(y_done, NT)
            pool.wait_ge(xst_ready, NT + 1)
            pool.wait_ge(bt_ready, GROUPS + 1)
            pool.dma_start(xr[:], xt_dram.rearrange("p (t n) -> p t n", t=NT)).then_inc(xr_in, 16)
            pool.wait_ge(hout_out, 16 * NT)
            v = st.inc(pool.memset(acc2[:], 0.0))
            pool.wait_ge(pool_step, v)

            def square_pair(t0):
                plain()
                v = st.inc(pool.tensor_tensor(sq2[:], mix[:, ds(t0, 2), :], mix[:, ds(t0, 2), :], ALU.mult))
                pool.wait_ge(pool_step, v)
                plain()
                v = st.inc(pool.tensor_tensor(acc2[:], acc2[:], sq2[:], ALU.add))
                pool.wait_ge(pool_step, v)

            with pool.Fori(0, 8) as r:
                st.enter(r, 0, 2)
                pool.wait_ge(read_dve, 8 + r + 1)
                square_pair(2 * r)
                st.leave(8)
            pool.sem_inc(acc_done, 1)
            pool.wait_ge(rms_mm, 1)
            pool.wait_ge(acc_done, 1)
            v = st.inc(pool.memset(acc2[:], 0.0))
            pool.wait_ge(pool_step, v)
            for r in range(8):
                pool.wait_ge(x1_done, 2 * r + 2)
                square_pair(2 * r)
            pool.sem_inc(acc_done, 1)
            pool.wait_ge(rms_mm, 2)
            pool.wait_ge(acc_done, 2)
            v = st.inc(pool.memset(acc2[:], 0.0))
            pool.wait_ge(pool_step, v)
            for r in range(8):
                pool.wait_ge(read_dve, 32 + r + 1)
                v = st.inc(pool.tensor_tensor(sq2[:], ya[:, 2 * r:2 * r + 2, :], ya[:, 2 * r:2 * r + 2, :],
                                              ALU.mult))
                pool.wait_ge(pool_step, v)
                v = st.inc(pool.tensor_tensor(acc2[:], acc2[:], sq2[:], ALU.add))
                pool.wait_ge(pool_step, v)
            pool.sem_inc(acc_done, 1)
            pool.wait_ge(old_rows, 16)
            pool.wait_ge(vout, 2 * 16 * 8)
            pool.wait_ge(xout, 2 * 16 * 6)

        @block.scalar
        def _(act):
            def root(out, mean_square):
                act.activation(out, mean_square, ACT.Sqrt, bias=eps[:, 0:1]).then_inc(rooted, 1)

            def expect_root():
                act.activation(eps[0:1, 1:2], eps[0:1, 0:1], ACT.Sqrt)

            def split(pair, kq, width=256):
                act.wait_ge(raw_ready[kq], 16 * (pair + 1))
                if not (isinstance(pair, int) and pair == 0):
                    act.wait_ge(weights_used, 4 * pair + kq - 3)
                act.activation(whi[:, kq, :, 0:width], raw[:, kq, :, 0:width], ACT.Copy).then_inc(hi_done, 1)

            def ahead(pair0, i, c):
                split(pair0 + 2 * i + (c + 2) // 4, (c + 2) % 4)

            act.dma_start(prow[R_CONV:R_CONV + TAPS, :], conf_conv_w[0]).then_inc(par_in, 16)
            for r, w in ((R_CB, conf_conv_b), (R_NW, conf_norm_w), (R_NB, conf_norm_b), (R_SSD, ssd_norm_w),
                         (R_PREMIX, norm_pre_mix), (R_POSTMIX, norm_post_mix), (R_PREMLP, norm_pre_mlp),
                         (R_POSTMLP, norm_post_mlp)):
                act.dma_start(prow[r:r + 1, :], w).then_inc(par_in, 16)
            act.dma_start(prow[R_XW:R_XW + XTAPS, :], ssd_conv_w[0, :, 0:D]).then_inc(par_in, 16)
            act.dma_start(prow[R_XB:R_XB + 1, :], ssd_conv_b[:, 0:D]).then_inc(par_in, 16)
            act.dma_start(dsk[:], d_skip).then_inc(dsk_in, 16)
            act.dma_start(prow2[0:XTAPS, :], ssd_conv_w[0, :, D:D_XBC]).then_inc(par_in, 16)
            act.dma_start(prow2[XTAPS:XTAPS + 1, :], ssd_conv_b[:, D:D_XBC]).then_inc(par_in, 16)
            act.wait_ge(consts, 3)
            for c in range(3):
                n = P if c < 2 else NB * DS
                junk = xt0[0:n, :, :].rearrange("p a b -> p (a b)")[:, 0:D]
                act.wait_ge(x_in[c], 16)
                if c:
                    act.wait_ge(ss_done, c)
                act.activation(junk, xn[0:n, c, :], ACT.Square, accum_out=ss[0:n, c:c + 1]).then_inc(ss_done, 1)
            act.wait_ge(ss_done, 3)
            act.activation(ss[:, 0:3], ss[:, 0:3], ACT.Sqrt, bias=eps[:, 0:1], scale=1.0 / D).then_inc(rooted, 1)
            act.wait_ge(par_trans, 1)
            act.activation(par[:, 0:8, :], ps[:, 5, 0:8 * NROW].rearrange("p (t r) -> p t r", t=8), ACT.Copy)
            act.activation(par[:, 8:16, :], ps[:, 6, 0:8 * NROW].rearrange("p (t r) -> p t r", t=8), ACT.Copy)
            act.activation(sw[:, NT:NX, :], ps[:, 6, 360:400].rearrange("p (t r) -> p t r", t=8), ACT.Copy
                           ).then_inc(par_copied, 1)
            act.wait_ge(par_copied, 1)
            act.activation(sw[:, 0:NT, :], par[:, :, R_XW:R_XB + 1], ACT.Copy).then_inc(par_done, 1)
            act.wait_ge(rb_mm, 1)
            act.activation(rb[:], ps[:, 4, 0:TOK], ACT.Copy).then_inc(rb_done, 1)
            split(Q_DT, 0, P)
            split(Q_DT, 1, P)
            act.wait_ge(par_done, 1)
            def keep_x(t):
                act.wait_ge(x_trans, t + 1)
                act.activation(xt0[:, t, :], ps[:, t % 4, 0:TOK], ACT.Copy).then_inc(x_copied, 1)

            keep_x(0)
            for t in range(NT):
                if t + 1 < NT:
                    keep_x(t + 1)
                act.wait_ge(t1_done, t + 1)
                act.activation(ahi[:, t, :], t1[:, t % 2, :], ACT.Copy, scale=par[:, t, R_PREMIX:R_PREMIX + 1]
                               ).then_inc(ahi_done, 1)
            act.wait_ge(x_copied, NT)
            act.dma_start(xt_dram.rearrange("p (t n) -> p t n", t=NT), xt0[:]).then_inc(xt_stored, 16)
            split(Q_DT, 2, P)
            split(Q_DT, 3, P)
            split(Q_GLU, 0)
            split(Q_GLU, 1)

            def conv_states(batch):
                act.wait_ge(xt_stored, 16)
                for t in range(2 * batch, 2 * batch + 2):
                    act.wait_ge(cst_trans, t + 1)
                    act.activation(v_sample1(t, 0, HALO), ps[:, 6 + t % 2, 0:NB * HALO].rearrange(
                        "p (b j) -> p b j", b=NB), ACT.Copy).then_inc(cst_done, 1)

            def xconv_states(h):
                act.wait_ge(sst_trans, h + 1)
                act.activation(xs[:, 12 * h:12 * h + 12, :], ps[:, 5, 0:288].rearrange("p (t r) -> p t r", t=12),
                               ACT.Copy).then_inc(sst_done, 1)

            def dt_part(c):
                if c == 0:
                    act.wait_ge(weights_used, 4)
                    act.wait_ge(dcol_in, 32)
                    act.activation(hw[:, 0, :], ps[0:HEADS, 4, 0:TOK], ACT.Identity, bias=dcol[:, 0:1]
                                   ).then_inc(dt_act, 1)
                if c == 1:
                    act.wait_ge(dt_dve, 1)
                    act.activation(hw[:, 1, :], hw[:, 2, :], ACT.Exp, scale=-1.0)
                    act.activation(dcol[:, 1:2], dcol[:, 1:2], ACT.Exp).then_inc(dt_act, 1)
                if c == 3:
                    act.wait_ge(dt_dve, 2)
                    act.activation(hw[:, 6, :], hw[:, 5, :], ACT.Exp)
                    act.activation(hw[:, 7, :], hw[:, 4, :], ACT.Exp).then_inc(dt_act, 1)
                if c == 7:
                    act.wait_ge(dt_trans, 1)
                    act.activation(tcol[:], ps[:, 4, 0:288].rearrange("p (c r) -> p c r", c=3), ACT.Copy
                                   ).then_inc(dt_ready, 1)

            def sigmoid(i):
                act.wait_ge(weights_used, 4 * (Q_GLU + 2 * i) + 4)
                if not (isinstance(i, int) and i == 0):
                    act.wait_ge(read_dve, i)
                act.activation(sg[:], gemm_bank(0), ACT.Sigmoid).then_inc(read_act, 1)

            def v_rows(i):
                act.wait_ge(vt_done, i + 1)
                if not (isinstance(i, int) and i == 0):
                    act.wait_ge(vout, 32 * i)
                act.activation(vtok[:], ps[0:VNEW, 5, 0:256], ACT.Copy).then_inc(vtok_ready, 1)

            def conv_begin(j):
                act.wait_ge(conv_turn, j + 1)
                for e, k in ((0, TAPS - 1), (1, TAPS - 2)):
                    w = par[:, j, R_CONV + k:R_CONV + k + 1]
                    func, b = (ACT.Copy, 0.0) if e else (ACT.Identity, par[:, j, R_CB:R_CB + 1])
                    act.activation(vacc[:, e, 0:SEQ], vx[:, j, k:k + SEQ], func, scale=w, bias=b)
                    last = act.activation(seqs(vacc[:, e, SEQ:TOK]), v_sample1(j, k, k + DS), func, scale=w,
                                          bias=b)
                last.then_inc(conv_begun, 1)

            def glu(i):
                for c in range(8):
                    ahead(Q_GLU, i, c)
                    if c == 0 and not (isinstance(i, int) and i == 0):
                        act.wait_ge(read_dve, i)
                        conv_begin(i - 1)
                    if isinstance(i, int) and i == 0:
                        dt_part(c)
                        conv_states(c)
                        if c in (2, 4):
                            xconv_states(c // 2 - 1)
                    if c == 3:
                        sigmoid(i)
                    if c == 5 and not (isinstance(i, int) and i == 0):
                        v_rows(i - 1)

            glu(0)
            with act.Fori(1, 8) as i:
                glu(i)

            def xbc_evac(i, p):
                r = 2 * i + p
                act.wait_ge(weights_used, 4 * (Q_XBC + r) + 4)
                if not (isinstance(i, int) and i == 0):
                    act.wait_ge(xconv_done, r - 1)
                    act.wait_ge(xw_ready, r - 1)
                buf = xe[:, p, :, XPEXT:XLEN].rearrange("p n (b j) -> p n b j", b=NB)
                act.activation(buf[:, :, :, 0:XHALO],
                               xs[:, ds(4 * i + 2 * p, 2), :].rearrange("p n (b j) -> p n b j", b=NB), ACT.Copy)
                act.activation(xe[:, p, :, XHALO:XPEXT], ps[:, 2 * p:2 * p + 2, 0:SEQ], ACT.Copy)
                for n in range(2):
                    t = 4 * i + 2 * p + n
                    act.activation(xb[:, t, :], ps[:, 2 * p + n, 0:TOK], ACT.Identity,
                                   scale=sw[:, t, XTAPS - 1:XTAPS], bias=sw[:, t, XTAPS:XTAPS + 1])
                act.activation(buf[:, :, :, XHALO:XSEXT],
                               ps[:, 2 * p:2 * p + 2, SEQ:TOK].rearrange("p n (b j) -> p n b j", b=NB),
                               ACT.Copy).then_inc(read_act, 1)

            def xbc_silu(i, p):
                act.wait_ge(xconv_done, 2 * i + p + 1)
                act.sem_inc(act_turn, 1)
                t = xb[:, ds(4 * i + 2 * p, 2), :]
                act.activation(t, t, ACT.Silu).then_inc(xb_done, 1)

            def x_rows(i):
                act.wait_ge(xwt_done, i + 1)
                if not (isinstance(i, int) and i == 0):
                    act.wait_ge(xout, 32 * i)
                act.activation(xtok[:], ps[0:XNEW, 5, :], ACT.Copy).then_inc(xtok_ready, 1)

            def xbc(i):
                first = isinstance(i, int) and i == 0
                for c in range(8):
                    ahead(Q_XBC, i, c)
                    if c == 0:
                        conv_begin(7 + i)
                    if c == 1 and not first:
                        xbc_silu(i - 1, 1)
                    if c == 3:
                        xbc_evac(i, 0)
                    if c == 5:
                        xbc_silu(i, 0)
                        if first:
                            v_rows(7)
                        else:
                            x_rows(i - 1)
                    if c == 7:
                        xbc_evac(i, 1)

            act.wait_ge(sst_done, 2)
            xbc(0)
            with act.Fori(1, 6) as i:
                xbc(i)

            def z_silu(i, p):
                act.wait_ge(weights_used, 4 * (Q_Z + 2 * i + p) + 4)
                act.activation(zg[:, ds(4 * i + 2 * p, 2), :], gemm_bank(p), ACT.Silu).then_inc(read_act, 1)

            def z(i):
                for c in range(8):
                    ahead(Q_Z, i, c)
                    if c == 0:
                        conv_begin(13 + i)
                    if isinstance(i, int) and i == 0 and c == 1:
                        xbc_silu(5, 1)
                    if isinstance(i, int) and i == 0 and c == 5:
                        x_rows(5)
                    if c == 3:
                        z_silu(i, 0)
                    if c == 7:
                        z_silu(i, 1)

            def square_group(gg):
                act.wait_ge(cent_done, gg + 1)
                if gg:
                    act.wait_ge(sq_summed, gg)
                act.activation(sqb[:, :, 0:SEQ], v_prompt(4 * gg, 4, 0, SEQ), ACT.Square)
                for n in range(4):
                    last = act.activation(seqs(sqb[:, n, SEQ:TOK]), v_sample1(4 * gg + n, 0, DS), ACT.Square)
                last.then_inc(sq_ready, 1)

            z(0)
            with act.Fori(1, 3) as i:
                z(i)
            for c in range(8):
                ahead(Q_Z, 3, c)
                if c == 0:
                    act.wait_ge(mean_mm, 1)
                    act.activation(rb[:], ps[:, 4, 0:TOK], ACT.Copy).then_inc(mean_done, 1)
                if c == 3:
                    z_silu(3, 0)
                if 2 <= c <= 5:
                    square_group(c - 2)

            expect_root()
            act.wait_ge(sq_used, 4)
            root(rb[:], ps[:, 4, 0:TOK])

            def conf_silu(t):
                w, b = par[:, t, R_NW:R_NW + 1], par[:, t, R_NB:R_NB + 1]
                act.wait_ge(cn_done, t // 4 + 1)
                act.activation(vx[:, t, 0:SEQ], vx[:, t, 0:SEQ], ACT.Silu, bias=b, scale=w)
                act.activation(v_sample1(t, 0, DS), v_sample1(t, 0, DS), ACT.Silu, bias=b, scale=w
                               ).then_inc(silu_done, 1)

            for t in range(NT):
                conf_silu(t)
                if t == 3:
                    z_silu(3, 1)

            def stage_x(T):
                if not (isinstance(T, int) and T == 0):
                    act.wait_ge(xtile_trans, T)
                act.activation(xst[:], xb[:, T, :], ACT.Copy).then_inc(xst_ready, 1)

            def stage_b(i):
                if not (isinstance(i, int) and i == 0):
                    act.wait_ge(cb_done, i)
                act.activation(bt[:], xb[:, NT + i, :], ACT.Copy).then_inc(bt_ready, 1)

            def load_h0(T, slot):
                act.dma_start(h0[:, slot], state_ssm[0].rearrange("b (t e) p n -> (e p) t b n", e=2)[:, T]
                              ).then_inc(h0_in[slot], 16)

            def store_h(T):
                act.wait_ge(hnew_done, T + 1)
                act.dma_start(s_ssm[0].rearrange("b (t e) p n -> (e p) t b n", e=2)[:, T], hout[:]
                              ).then_inc(hout_out, 16)
                act.wait_ge(pst_done, T + 1)
                act.dma_start(p_ssm[0, 0].rearrange("(t e) p n -> (e p) t n", e=2)[:, T], pst[:]
                              ).then_inc(pst_out, 16)

            def wc(i, final=False):
                for j in range(4):
                    T = 4 * i + j
                    first = isinstance(i, int) and i == 0 and j == 0
                    ahead(Q_WC, i, 2 * j)
                    if j == 0:
                        act.wait_ge(bt_trans, i + 1)
                        act.activation(btok[:], ps[:, 4, 0:384].rearrange("p (c n) -> p c n", c=3), ACT.Copy
                                       ).then_inc(btok_ready, 1)
                    act.wait_ge(seg_done, 2 * T + 1)
                    if not first:
                        act.wait_ge(y_done, T)
                    act.activation(wgt[:, 0, :], ps[:, 3, 0:TOK], ACT.Exp).then_inc(exp_done, 1)
                    act.wait_ge(h0_trans, T + 1)
                    act.activation(h0t[:, 0:4, :], ps[:, 6, :].rearrange("p (b n) -> p b n", b=4), ACT.Copy)
                    act.activation(h0t[:, 4:8, :], ps[:, 7, :].rearrange("p (b n) -> p b n", b=4), ACT.Copy
                                   ).then_inc(h0t_ready, 1)
                    if not first:
                        act.wait_ge(hnew_done, T)
                    if not (final and j == 3):
                        load_h0(T + 1, (j + 1) % 2)
                    ahead(Q_WC, i, 2 * j + 1)
                    act.wait_ge(ecb_mm, T + 1)
                    if not first:
                        act.wait_ge(y_read, T)
                    act.activation(ecb[:], ps[:, 2, TOK:512], ACT.Copy).then_inc(ecb_ready, 1)
                    act.wait_ge(seg_done, 2 * T + 2)
                    act.activation(wgt[:, 1, :], ps[:, 3, 0:TOK], ACT.Exp).then_inc(exp_done, 1)
                    act.wait_ge(pstart_done, T + 1)
                    act.activation(hts[:], ps[:, 4, 384:512], ACT.Copy).then_inc(hts_ready, 1)
                    if j % 2:
                        p = j // 2
                        act.wait_ge(weights_used, 4 * (Q_WC + 2 * i + p) + 4)
                        act.activation(mix[:, ds(4 * i + 2 * p, 2), :], gemm_bank(0), ACT.Copy
                                       ).then_inc(read_act, 1)
                    if j == 3:
                        stage_b(i + 1)
                    stage_x(T + 1)
                    store_h(T)

            act.wait_ge(act_ready, 2 * NT)
            act.wait_ge(dt_ready, 1)
            act.wait_ge(xb_done, 12)
            stage_b(0)
            stage_x(0)
            act.wait_ge(sq_used, 4)
            act.wait_ge(msum_done, 1)
            act.wait_ge(vout, 2 * 16 * 8)
            act.wait_ge(xout, 2 * 16 * 6)
            load_h0(0, 0)
            wc(0)
            with act.Fori(1, 3) as i:
                wc(i)
            wc(3, final=True)

            expect_root()
            act.wait_ge(gn_mm, 1)
            act.activation(gss[:], ps[:, 2:6, 0:TOK], ACT.Sqrt, bias=eps[:, 0:1], scale=float(GROUPS)
                           ).then_inc(rooted, 1)
            for t in range(NT):
                act.wait_ge(gn_done, t // 4 + 1)
                act.wait_ge(weights_used, 4 * Q_WS)
                act.activation(ahi[:, t, :], zg[:, t, :], ACT.Copy, scale=par[:, t, R_SSD:R_SSD + 1]
                               ).then_inc(ahi_done, 1)

            with act.Fori(0, 4) as i:
                for c in range(8):
                    ahead(Q_WS, i, c)

            expect_root()
            act.wait_ge(rms_mm, 1)
            root(rb[:], ps[:, 4, 0:TOK])
            for t in range(NT):
                act.wait_ge(x1_done, t + 1)
                act.activation(ahi[:, t, :], mix[:, t, :], ACT.Copy, scale=par[:, t, R_PREMLP:R_PREMLP + 1]
                               ).then_inc(ahi_done, 1)

            act.wait_ge(hout_out, 16 * NT)
            act.wait_ge(pst_out, 16 * NT)

            def up(q, i, start=False):
                for c in range(8):
                    ahead(q_up(q), i, c)
                    if start and c == 1:
                        act.wait_ge(rms_mm, 2)
                        root(rb2[:], ps[:, 5, 0:TOK])
                    if c % 4 == 3:
                        p = c // 4
                        n = 8 * q + 2 * i + p
                        act.wait_ge(rh_done, n + 1)
                        act.activation(hs[:], rh[:], ACT.Square).then_inc(hs_done, 1)
                        act.wait_ge(hs_done, n + 1)
                        act.activation(hhi[:, ds(4 * i + 2 * p, 2), :], hs[:], ACT.Copy).then_inc(hhi_done, 1)

            def down(q, i, last=False):
                for c in range(8):
                    if not (last and c >= 6):
                        ahead(q_down(q), i, c)
                    if c % 4 == 3 and isinstance(q, int) and q == 0:
                        p = c // 4
                        act.wait_ge(weights_used, 4 * (q_down(q) + 2 * i + p) + 4)
                        act.activation(ya[:, ds(4 * i + 2 * p, 2), :], gemm_bank(p), ACT.Copy
                                       ).then_inc(read_act, 1)

            up(0, 0, start=True)
            with act.Fori(1, 4) as i:
                up(0, i)
            with act.Fori(0, 4) as i:
                down(0, i)
            with act.Fori(1, 3) as q:
                with act.Fori(0, 4) as i:
                    up(q, i)
                with act.Fori(0, 4) as i:
                    down(q, i)
            with act.Fori(0, 4) as i:
                up(3, i)
            with act.Fori(0, 3) as i:
                down(3, i)
            down(3, 3, last=True)

            expect_root()
            act.wait_ge(rms_mm, 3)
            root(rb[:], ps[:, 4, 0:TOK])
            for g in range(4):
                act.wait_ge(ot_trans, g + 1)
                b = 3 * (g % 2)
                act.activation(yo[:, 0:2, 512 * g:512 * g + 512], ps[:, b:b + 2, :], ACT.Copy)
                act.activation(yo[0:NB * DS, 2, 512 * g:512 * g + 512], ps[0:NB * DS, b + 2, :], ACT.Copy
                               ).then_inc(ot_copied, 1)
                act.wait_ge(ot_copied, g + 1)
                col = slice(512 * g, 512 * g + 512)
                act.dma_start(y_prompt[0].rearrange("(c p) d -> p c d", p=P)[:, :, col], yo[:, 0:2, col]
                              ).then_inc(y_out, 16)
                act.dma_start(y_sample.rearrange("b s d -> (b s) d")[:, col], yo[0:NB * DS, 2, col]
                              ).then_inc(y_out, 16)
            act.wait_ge(xt_stored, 16)
            act.wait_ge(hout_out, 16 * NT)
            act.wait_ge(pst_out, 16 * NT)
            act.wait_ge(y_out, 2 * 16 * 4)

        @block.vector
        def _(dve):
            st = Steps(dve_step)

            def split(pair, kq, width=256):
                dve.wait_ge(hi_done, 4 * pair + kq + 1)
                dve.tensor_tensor(wlo[:, kq, :, 0:width], raw[:, kq, :, 0:width],
                                  whi[:, kq, :, 0:width].bitcast(F32), ALU.subtract).then_inc(lo_done[kq], 1)

            def ahead(pair0, i, c, shared=False):
                if shared and c % 2:
                    return
                split(pair0 + 2 * i + (c + 2) // 4, (c + 2) % 4)

            dve.memset(vacc[:], 0.0).then_inc(conv_turn, 1)
            dve.wait_ge(dsk_in, 16)
            dve.tensor_copy(prow[R_DSKIP:R_DSKIP + 1, :].rearrange("a (h p) -> a h p", p=HD),
                            dsk[:].unsqueeze(2).to_broadcast([1, HEADS, HD])).then_inc(dsk_done, 1)
            dve.wait_ge(rooted, 1)
            dve.wait_ge(consts, 3)
            dve.wait_ge(dve_step, st.inc(dve.reciprocal(ss[:, 0:3], ss[:, 0:3])))
            for c in range(3):
                last = dve.tensor_scalar(diag[:, c, :], ident[:], ss[:, c:c + 1], None, ALU.mult)
            last.then_inc(diag_done, 1)
            split(Q_DT, 0, P)
            split(Q_DT, 1, P)

            def in_lo(t):
                dve.wait_ge(ahi_done, t + 1)
                dve.scalar_tensor_tensor(out=alo[:, t, :], in0=t1[:, t % 2, :],
                                         scalar=par[:, t, R_PREMIX:R_PREMIX + 1],
                                         in1=ahi[:, t, :].bitcast(F32), op0=ALU.mult, op1=ALU.subtract
                                         ).then_inc(act_ready, 1)

            dve.wait_ge(rb_done, 1)
            dve.wait_ge(par_done, 1)
            for t in range(NT):
                dve.wait_ge(x_copied, t + 1)
                if t >= 2:
                    dve.wait_ge(act_ready, t - 1)
                dve.tensor_tensor(t1[:, t % 2, :], ps[:, t % 4, 0:TOK], rb[:], ALU.mult).then_inc(t1_done, 1)
                if t:
                    in_lo(t - 1)
            in_lo(NT - 1)
            split(Q_DT, 2, P)
            split(Q_DT, 3, P)
            split(Q_GLU, 0)
            split(Q_GLU, 1)

            def chain(ins):
                dve.wait_ge(dve_step, st.inc(ins))

            X, E, A, S2, CUM, DL, DTE, ECUM = range(8)

            def row(r):
                return hw[:, r, :]

            def dt_part(c):
                if c == 0:
                    dve.wait_ge(dt_act, 1)
                    chain(dve.scalar_tensor_tensor(out=row(A), in0=row(X), scalar=-1.0, in1=row(X),
                                                   op0=ALU.mult, op1=ALU.max))
                    dve.tensor_scalar(row(DTE), row(X), 0.0, None, ALU.max)
                    dve.memset(row(CUM), 1.0).then_inc(dt_dve, 1)
                    dve.wait_ge(dt_dve, 1)
                    for k in range(2):
                        dve.memset(hw[:, CUM, k * P:k * P + 1], 0.0)
                    chain(dve.memset(seqs(hw[:, CUM, SEQ:TOK])[:, :, 0:1], 0.0))
                if c == 1:
                    dve.wait_ge(dt_act, 2)
                    chain(dve.tensor_scalar(row(A), row(E), 2.0, None, ALU.add))
                    chain(dve.reciprocal(row(A), row(A)))
                    chain(dve.tensor_tensor(row(E), row(E), row(A), ALU.mult))
                    chain(dve.tensor_tensor(row(S2), row(E), row(E), ALU.mult))
                    chain(dve.tensor_scalar(row(A), row(S2), 1.0 / 17.0, None, ALU.mult))
                if c == 2:
                    for n in (15, 13, 11, 9, 7, 5, 3):
                        chain(dve.scalar_tensor_tensor(out=row(A), in0=row(A), scalar=1.0 / n, in1=row(S2),
                                                       op0=ALU.add, op1=ALU.mult))
                if c == 3:
                    chain(dve.scalar_tensor_tensor(out=row(A), in0=row(A), scalar=1.0, in1=row(E),
                                                   op0=ALU.add, op1=ALU.mult))
                    chain(dve.scalar_tensor_tensor(out=row(X), in0=row(A), scalar=2.0, in1=row(DTE),
                                                   op0=ALU.mult, op1=ALU.add))
                    chain(dve.tensor_scalar(row(A), row(X), dcol[:, 1:2], -1.0, ALU.mult, ALU.mult))
                    chain(dve.tensor_tensor_scan(out=row(E), data0=row(CUM), data1=row(A), initial=0.0,
                                                 op0=ALU.mult, op1=ALU.add))
                    dve.tensor_copy(row(CUM), row(E))
                    for k in range(2):
                        dve.tensor_tensor(hw[:, DL, k * P:(k + 1) * P],
                                          hw[:, E, k * P + P - 1:k * P + P].to_broadcast([HEADS, P]),
                                          hw[:, E, k * P:(k + 1) * P], ALU.subtract)
                    dve.tensor_tensor(seqs(hw[:, DL, SEQ:TOK]),
                                      seqs(hw[:, E, SEQ:TOK])[:, :, DS - 1:DS].to_broadcast([HEADS, NB, DS]),
                                      seqs(hw[:, E, SEQ:TOK]), ALU.subtract).then_inc(dt_dve, 1)
                if c == 4:
                    dve.wait_ge(dt_act, 3)
                    dve.wait_ge(dt_dve, 2)
                    chain(dve.tensor_tensor(row(DTE), row(DTE), row(X), ALU.mult))
                    dve.tensor_copy(hst[0:32, :], row(E))
                    dve.tensor_copy(hst[32:64, :], row(X))
                    dve.tensor_copy(hst[64:96, :], row(DTE)).then_inc(dt_dve, 1)
                if c in (5, 6):
                    r, dst = ((E, cum3), (ECUM, ecum3))[c - 5]
                    if c == 5:
                        dve.wait_ge(dt_dve, 3)
                    chain(dve.tensor_copy(hb[:, 0, :], row(r)))
                    chain(dve.tensor_tensor(row(r), row(r), hb[:, 0, :], ALU.subtract))
                    chain(dve.tensor_copy(hb[:, 1, :], row(r)))
                    chain(dve.tensor_tensor(row(r), row(r), hb[:, 1, :], ALU.subtract))
                    chain(dve.tensor_copy(hb[:, 2, :], row(r)))
                    for part in range(3):
                        last = dve.tensor_copy(dst[32 * part:32 * part + 32, :], hb[:, part, :])
                    chain(last)

            def make_v(i):
                dve.wait_ge(weights_used, 4 * (Q_GLU + 2 * i + 1) + 4)
                dve.wait_ge(read_act, i + 1)
                dve.tensor_tensor(v_prompt(2 * i, 2, HALO, PEXT), ps[:, 2:4, 0:SEQ], sg[:, :, 0:SEQ], ALU.mult)
                for n in range(2):
                    last = dve.tensor_tensor(v_sample1(2 * i + n, HALO, SEXT), seqs(ps[:, 2 + n, SEQ:TOK]),
                                             seqs(sg[:, n, SEQ:TOK]), ALU.mult)
                last.then_inc(read_dve, 1)
                dve.wait_ge(read_dve, i + 1)

            CUTS = [29, 29, 25, 21, 17, 13, 9, 4, 0]
            part_at = [0] * 4

            def conv(j, c):
                if c == 0:
                    return
                if c == 1:
                    dve.wait_ge(conv_begun, j + 1)
                for k in range(CUTS[c] - 1, CUTS[c + 1] - 1, -1):
                    e = k % 2
                    acc = (vacc[:, e, 0:SEQ], seqs(vacc[:, e, SEQ:TOK]))
                    src = (vx[:, j, k:k + SEQ], v_sample1(j, k, k + DS))
                    for s in range(2):
                        if k < TAPS - 4:
                            dve.wait_ge(dve_step, part_at[2 * e + s])
                        part_at[2 * e + s] = st.inc(dve.scalar_tensor_tensor(
                            out=acc[s], in0=src[s], scalar=par[:, j, R_CONV + k:R_CONV + k + 1], in1=acc[s],
                            op0=ALU.mult, op1=ALU.add))
                if c == 7:
                    dve.wait_ge(dve_step, part_at[0])
                    st.inc(dve.tensor_tensor(vx[:, j, 0:SEQ], vacc[:, 0, 0:SEQ], vacc[:, 1, 0:SEQ], ALU.add))
                    dve.wait_ge(dve_step, part_at[1])
                    dve.tensor_tensor(v_sample1(j, 0, DS), seqs(vacc[:, 0, SEQ:TOK]), seqs(vacc[:, 1, SEQ:TOK]),
                                      ALU.add).then_inc(conv_turn, 1)

            CONV_STEPS = 2 * (TAPS - 2) + 1

            def glu(i):
                for c in range(8):
                    ahead(Q_GLU, i, c, shared=True)
                    if isinstance(i, int) and i == 0:
                        dt_part(c)
                        if c == 7:
                            dve.wait_ge(halo_zero, 1)
                            dve.wait_ge(cst_done, NT)
                    else:
                        conv(i - 1, c)
                    if c == 7:
                        make_v(i)

            glu(0)
            with dve.Fori(1, 8) as i:
                st.enter(i, 1, CONV_STEPS)
                glu(i)
                st.leave(7)

            def xconv(i, p):
                dve.wait_ge(read_act, 8 + 2 * i + p + 1)
                last_at = [0] * 4
                for k in range(XTAPS - 2, -1, -1):
                    for n in range(2):
                        t = 4 * i + 2 * p + n
                        src = (xe[:, p, n, k:k + SEQ], seqs(xe[:, p, n, XPEXT:XLEN])[:, :, k:k + DS])
                        dst = (xb[:, t, 0:SEQ], seqs(xb[:, t, SEQ:TOK]))
                        w = sw[:, t, k:k + 1]
                        for s in range(2):
                            if k < XTAPS - 2:
                                dve.wait_ge(dve_step, last_at[2 * n + s])
                            ins = dve.scalar_tensor_tensor(out=dst[s], in0=src[s], scalar=w, in1=dst[s],
                                                           op0=ALU.mult, op1=ALU.add)
                            if k == 0 and n == 1 and s == 1:
                                ins.then_inc(xconv_done, 1)
                            else:
                                last_at[2 * n + s] = st.inc(ins)

            XCONV_STEPS = 4 * (XTAPS - 1) - 1

            def xbc(i):
                for c in range(8):
                    ahead(Q_XBC, i, c, shared=True)
                    conv(7 + i, c)
                    if c == 3:
                        xconv(i, 0)
                    if c == 7:
                        xconv(i, 1)

            xbc(0)
            with dve.Fori(1, 6) as i:
                st.enter(i, 1, CONV_STEPS + 2 * XCONV_STEPS)
                xbc(i)
                st.leave(5)

            def z(i):
                for c in range(8):
                    ahead(Q_Z, i, c, shared=True)
                    conv(13 + i, c)

            z(0)
            with dve.Fori(1, 3) as i:
                st.enter(i, 1, CONV_STEPS)
                z(i)
                st.leave(2)

            def on_group(gg, op, sem_):
                v = v_prompt(4 * gg, 4, 0, SEQ)
                dve.tensor_tensor(v, v, rb[:, 0:SEQ].unsqueeze(1).to_broadcast([P, 4, SEQ]), op)
                v = v_sample(4 * gg, 4, 0, DS)
                dve.tensor_tensor(v, v, seqs(rb[:, SEQ:TOK]).unsqueeze(1).to_broadcast([P, 4, NB, DS]), op
                                  ).then_inc(sem_, 1)

            for c in range(8):
                ahead(Q_Z, 3, c, shared=True)
                if c == 0:
                    dve.wait_ge(mean_done, 1)
                    dve.wait_ge(conv_turn, NT + 1)
                    dve.wait_ge(msum_done, 1)
                if c <= 3:
                    on_group(c, ALU.subtract, cent_done)
                if 3 <= c <= 6:
                    dve.wait_ge(sq_ready, c - 2)
                    if c > 3:
                        dve.wait_ge(sq_used, c - 3)
                    dve.tensor_reduce(sqs[:], sqb[:].rearrange("p n t -> p t n"), axis=mybir.AxisListType.X,
                                      op=ALU.add).then_inc(sq_summed, 1)
            dve.wait_ge(rooted, 2)
            dve.reciprocal(rb[:], rb[:]).then_inc(var_root, 1)
            dve.wait_ge(var_root, 1)
            for gg in range(4):
                on_group(gg, ALU.mult, cn_done)
            for gg in range(4):
                if gg == 0:
                    dve.wait_ge(weights_used, 4 * Q_WC)
                dve.wait_ge(silu_done, 4 * gg + 4)
                t = 4 * gg
                dve.tensor_copy(ahi[:, t:t + 4, 0:SEQ], v_prompt(t, 4, 0, SEQ))
                dve.tensor_copy(ahi[:, t:t + 4, SEQ:TOK].rearrange("p n (b j) -> p n b j", b=NB),
                                v_sample(t, 4, 0, DS)).then_inc(ahi_done, 4)
                dve.wait_ge(ahi_done, NT + 4 * gg + 4)
                dve.tensor_tensor(alo[:, t:t + 4, 0:SEQ], v_prompt(t, 4, 0, SEQ),
                                  ahi[:, t:t + 4, 0:SEQ].bitcast(F32), ALU.subtract)
                dve.tensor_tensor(alo[:, t:t + 4, SEQ:TOK].rearrange("p n (b j) -> p n b j", b=NB),
                                  v_sample(t, 4, 0, DS),
                                  ahi[:, t:t + 4, SEQ:TOK].bitcast(F32).rearrange("p n (b j) -> p n b j", b=NB),
                                  ALU.subtract).then_inc(act_ready, 4)

            xt3 = ps[:, 4, 0:384].rearrange("p (c h d) -> p c h d", c=3, h=2)

            def wc(i):
                for j in range(4):
                    T = 4 * i + j
                    first = isinstance(i, int) and i == 0 and j == 0
                    ahead(Q_WC, i, 2 * j)
                    if j == 0:
                        dve.wait_ge(btok_ready, i + 1)
                        if not (isinstance(i, int) and i == 0):
                            dve.wait_ge(st_done, 4 * i)
                        dve.tensor_tensor(bm[:], btok[:, 2, :].unsqueeze(1).to_broadcast([P, NB, P]),
                                          blk[:].unsqueeze(2).to_broadcast([P, NB, P]), ALU.mult
                                          ).then_inc(bm_ready, 1)
                    dve.wait_ge(xtile_trans, T + 1)
                    if not first:
                        dve.wait_ge(y_done, T)
                    dve.tensor_tensor(xd[:].rearrange("p c (h d) -> p c h d", h=2), xt3,
                                      tcol[:, :, ds(HEADS + 2 * T, 2)].unsqueeze(3).to_broadcast([P, 3, 2, HD]),
                                      ALU.mult)
                    dve.tensor_tensor(xdd[:].rearrange("p c (h d) -> p c h d", h=2), xt3,
                                      tcol[:, :, ds(2 * HEADS + 2 * T, 2)].unsqueeze(3).to_broadcast([P, 3, 2, HD]),
                                      ALU.mult).then_inc(xd_ready, 1)
                    if j == 0:
                        dve.wait_ge(cb_done, i + 1)
                    dve.wait_ge(exp_done, 2 * T + 1)
                    dve.tensor_tensor(wgt[:, 0, :], ps[:, 2, 0:TOK], wgt[:, 0, :], ALU.mult).then_inc(mixw_done, 1)
                    ahead(Q_WC, i, 2 * j + 1)
                    dve.wait_ge(exp_done, 2 * T + 2)
                    dve.tensor_tensor(wgt[:, 1, :], ps[:, 2, 0:TOK], wgt[:, 1, :], ALU.mult).then_inc(mixw_done, 1)
                    dve.wait_ge(st_done, T + 1)
                    dve.wait_ge(ecb_ready, T + 1)
                    if not first:
                        dve.wait_ge(hout_out, 16 * T)
                        dve.wait_ge(pst_out, 16 * T)
                    for b in range(NB):
                        col = P + DS * b + DS - 1
                        last = dve.scalar_tensor_tensor(
                            out=hout[:, b, :], in0=h0[:, j % 2, b, :], scalar=ecb[:, col:col + 1],
                            in1=ps[:, 6 + b // 4, (b % 4) * P:(b % 4 + 1) * P], op0=ALU.mult, op1=ALU.add)
                    last.then_inc(hnew_done, 1)
                    v = st.inc(dve.tensor_scalar(s0s[:], ps[:, 4, 0:P], ecb[:, P - 1:P], None, ALU.mult))
                    dve.wait_ge(dve_step, v)
                    dve.tensor_tensor(pst[:], ps[:, 4, P:2 * P], s0s[:], ALU.add).then_inc(pst_done, 1)
                    dve.wait_ge(y_done, T + 1)
                    v1 = st.inc(dve.tensor_tensor(yoff[:], ps[:, 5, TOK:512], ecb[:], ALU.mult))
                    v2 = st.inc(dve.scalar_tensor_tensor(
                        out=ysum[:], in0=xb[:, T, :], scalar=par[:, T, R_DSKIP:R_DSKIP + 1],
                        in1=ps[:, 5, 0:TOK], op0=ALU.mult, op1=ALU.add))
                    dve.wait_ge(dve_step, v2)
                    dve.tensor_tensor(ysum[:, P:TOK], ysum[:, P:TOK], yoff[:], ALU.add).then_inc(y_read, 1)
                    dve.wait_ge(y_read, T + 1)
                    dve.tensor_tensor(zg[:, T, :], ysum[:], zg[:, T, :], ALU.mult).then_inc(g_done, 1)
                    dve.wait_ge(g_done, T + 1)

            WC_STEPS = 4 * 3
            dve.wait_ge(act_ready, 2 * NT)
            dve.wait_ge(dt_ready, 1)
            dve.wait_ge(read_act, 28)
            wc(0)
            with dve.Fori(1, 4) as i:
                st.enter(i, 1, WC_STEPS)
                wc(i)
                st.leave(3)

            dve.wait_ge(rooted, 3)
            for g in range(GROUPS):
                dve.reciprocal(gss[:, g, :], gss[:, g, :]).then_inc(gn_root, 1)
                dve.wait_ge(gn_root, g + 1)
                dve.tensor_tensor(zg[:, 4 * g:4 * g + 4, :], zg[:, 4 * g:4 * g + 4, :],
                                  gss[:, g, :].unsqueeze(1).to_broadcast([P, 4, TOK]), ALU.mult
                                  ).then_inc(gn_done, 1)
            for t in range(NT):
                dve.wait_ge(ahi_done, 2 * NT + t + 1)
                dve.scalar_tensor_tensor(out=alo[:, t, :], in0=zg[:, t, :], scalar=par[:, t, R_SSD:R_SSD + 1],
                                         in1=ahi[:, t, :].bitcast(F32), op0=ALU.mult, op1=ALU.subtract
                                         ).then_inc(act_ready, 1)

            with dve.Fori(0, 4) as i:
                for c in range(8):
                    ahead(Q_WS, i, c)
                    if c % 4 == 3:
                        p = c // 4
                        dve.wait_ge(weights_used, 4 * (Q_WS + 2 * i + p) + 4)
                        m = mix[:, ds(4 * i + 2 * p, 2), :]
                        dve.tensor_tensor(m, gemm_bank(p), m, ALU.add).then_inc(read_dve, 1)

            dve.wait_ge(rms_mm, 1)
            dve.wait_ge(rooted, 4)
            dve.reciprocal(rb[:], rb[:]).then_inc(rms_done, 1)
            dve.wait_ge(rms_done, 1)
            dve.wait_ge(xr_in, 16)
            dve.wait_ge(read_dve, 16)
            dve.wait_ge(hout_out, 16 * NT)
            for g in range(4):
                if g:
                    dve.wait_ge(x1_done, 4 * g)
                dve.tensor_tensor(t4[:], mix[:, 4 * g:4 * g + 4, :], rb[:].unsqueeze(1).to_broadcast([P, 4, TOK]),
                                  ALU.mult).then_inc(t4_done, 1)
                dve.wait_ge(t4_done, g + 1)
                for n in range(4):
                    t = 4 * g + n
                    dve.scalar_tensor_tensor(out=mix[:, t, :], in0=t4[:, n, :],
                                             scalar=par[:, t, R_POSTMIX:R_POSTMIX + 1], in1=xr[:, t, :],
                                             op0=ALU.mult, op1=ALU.add).then_inc(x1_done, 1)
                for n in range(4):
                    t = 4 * g + n
                    dve.wait_ge(ahi_done, 3 * NT + t + 1)
                    dve.scalar_tensor_tensor(out=alo[:, t, :], in0=mix[:, t, :],
                                             scalar=par[:, t, R_PREMLP:R_PREMLP + 1],
                                             in1=ahi[:, t, :].bitcast(F32), op0=ALU.mult, op1=ALU.subtract
                                             ).then_inc(act_ready, 1)

            dve.wait_ge(pst_out, 16 * NT)
            rbb = rb2[:].unsqueeze(1).to_broadcast([P, 2, TOK])

            def up(q, i, start=False):
                for c in range(8):
                    ahead(q_up(q), i, c)
                    if start and c == 1:
                        dve.wait_ge(rms_mm, 2)
                        dve.wait_ge(rooted, 5)
                        dve.reciprocal(rb2[:], rb2[:]).then_inc(rms_done, 1)
                        dve.wait_ge(rms_done, 2)
                    if c % 4 == 3:
                        p = c // 4
                        n = 8 * q + 2 * i + p
                        dve.wait_ge(weights_used, 4 * (q_up(q) + 2 * i + p) + 4)
                        dve.scalar_tensor_tensor(out=rh[:], in0=gemm_bank(p), scalar=0.0, in1=rbb,
                                                 op0=ALU.max, op1=ALU.mult).then_inc(rh_done, 1)
                        dve.wait_ge(hhi_done, n + 1)
                        dve.tensor_tensor(hlo[:, ds(4 * i + 2 * p, 2), :], hs[:],
                                          hhi[:, ds(4 * i + 2 * p, 2), :].bitcast(F32), ALU.subtract
                                          ).then_inc(hid_ready, 1)

            def down(q, i, last=False):
                for c in range(8):
                    if not (last and c >= 6):
                        ahead(q_down(q), i, c)
                    if c % 4 == 3 and not (isinstance(q, int) and q == 0):
                        p = c // 4
                        dve.wait_ge(weights_used, 4 * (q_down(q) + 2 * i + p) + 4)
                        m = ya[:, ds(4 * i + 2 * p, 2), :]
                        dve.tensor_tensor(m, gemm_bank(p), m, ALU.add).then_inc(read_dve, 1)

            up(0, 0, start=True)
            with dve.Fori(1, 4) as i:
                up(0, i)
            with dve.Fori(0, 4) as i:
                down(0, i)
            dve.wait_ge(read_act, 44)
            with dve.Fori(1, 3) as q:
                with dve.Fori(0, 4) as i:
                    up(q, i)
                with dve.Fori(0, 4) as i:
                    down(q, i)
                dve.wait_ge(read_dve, 8 * q + 16)
            with dve.Fori(0, 4) as i:
                up(3, i)
            with dve.Fori(0, 3) as i:
                down(3, i)
            down(3, 3, last=True)

            dve.wait_ge(rms_mm, 3)
            dve.wait_ge(rooted, 6)
            dve.reciprocal(rb[:], rb[:]).then_inc(rms_done, 1)
            dve.wait_ge(rms_done, 3)
            dve.wait_ge(read_dve, 40)
            for g in range(4):
                dve.wait_ge(x1_done, NT + 4 * g)
                dve.tensor_tensor(t4[:], ya[:, 4 * g:4 * g + 4, :], rb[:].unsqueeze(1).to_broadcast([P, 4, TOK]),
                                  ALU.mult).then_inc(t4_done, 1)
                dve.wait_ge(t4_done, 4 + g + 1)
                for n in range(4):
                    t = 4 * g + n
                    dve.scalar_tensor_tensor(out=mix[:, t, :], in0=t4[:, n, :],
                                             scalar=par[:, t, R_POSTMLP:R_POSTMLP + 1], in1=mix[:, t, :],
                                             op0=ALU.mult, op1=ALU.add).then_inc(x1_done, 1)

        @block.tensor
        def _(pe):
            def granule(pair, kq, bank, hi, lo, tiles=2):
                pe.wait_ge(lo_done[kq], pair + 1)
                for n in range(tiles):
                    out = ps[:, bank + n, 0:TOK]
                    for k in range(4):
                        kk = 4 * kq + k
                        wh, wl = whi[:, kq, k, n * P:(n + 1) * P], wlo[:, kq, k, n * P:(n + 1) * P]
                        pe.matmul(out, wh, hi[:, kk, :], start=(kk == 0), stop=False)
                        pe.matmul(out, wh, lo[:, kk, :], start=False, stop=False)
                        last = pe.matmul(out, wl, hi[:, kk, :], start=False, stop=(kk == NT - 1))
                last.then_inc(weights_used, 1)

            pe.wait_ge(consts, 3)
            pe.wait_ge(par_in, 16 * 13)
            pe.wait_ge(dsk_done, 1)
            for t in range(NT):
                pe.transpose(ps[:, 5 + t // 8, (t % 8) * NROW:(t % 8 + 1) * NROW], prow[:, t * P:(t + 1) * P],
                             ident[0:NROW, 0:NROW])
            for t in range(8):
                last = pe.transpose(ps[:, 6, 360 + 5 * t:365 + 5 * t], prow2[:, t * P:(t + 1) * P],
                                    ident[0:XTAPS + 1, 0:XTAPS + 1])
            last.then_inc(par_trans, 1)
            for c in range(3):
                pe.wait_ge(x_in[c], 16)

            def turn_x(t):
                if t >= 4:
                    pe.wait_ge(x_copied, t - 3)
                    pe.wait_ge(t1_done, t - 3)
                pe.transpose(ps[:, t % 4, 0:P], xn[:, 0, t * P:(t + 1) * P], ident[:])
                pe.transpose(ps[:, t % 4, P:SEQ], xn[:, 1, t * P:(t + 1) * P], ident[:])
                pe.transpose(ps[:, t % 4, SEQ:TOK], xn[0:64, 2, t * P:(t + 1) * P], ident[0:64, 0:64]
                             ).then_inc(x_trans, 1)

            for t in range(4):
                turn_x(t)
            pe.wait_ge(diag_done, 1)
            pe.matmul(ps[:, 4, 0:P], ones[:], diag[:, 0, :], start=True, stop=True)
            pe.matmul(ps[:, 4, P:SEQ], ones[:], diag[:, 1, :], start=True, stop=True)
            pe.matmul(ps[:, 4, SEQ:TOK], ones[:], diag[:, 2, 0:64], start=True, stop=True).then_inc(rb_mm, 1)
            for t in range(4, NT):
                turn_x(t)
            def turn_conv_states(batch):
                pe.wait_ge(par_done, 1)
                pe.wait_ge(cst_in, 32)
                for t in range(2 * batch, 2 * batch + 2):
                    if t >= 2:
                        pe.wait_ge(cst_done, t - 1)
                    for h in range(2):
                        last = pe.transpose(ps[:, 6 + t % 2, h * 120:h * 120 + 120], cst[:, h, t * P:(t + 1) * P],
                                            ident[0:120, 0:120])
                    last.then_inc(cst_trans, 1)

            def turn_xconv_states(h):
                pe.wait_ge(sst_in, 16)
                if h:
                    pe.wait_ge(sst_done, h)
                for t in range(12):
                    last = pe.transpose(ps[:, 5, t * 24:t * 24 + 24], sst[:, (12 * h + t) * P:(12 * h + t + 1) * P],
                                        ident[0:24, 0:24])
                last.then_inc(sst_trans, 1)

            pe.wait_ge(rb_done, 1)
            for kq in range(4):
                pe.wait_ge(act_ready, 4 * kq + 4)
                granule(Q_DT, kq, 4, ahi, alo, tiles=1)

            def turn_dt():
                pe.wait_ge(dt_dve, 3)
                for c, off in enumerate((0, P, TOK - P)):
                    last = pe.transpose(ps[:, 4, c * 96:(c + 1) * 96], hst[:, off:off + P], ident[0:96, 0:96])
                last.then_inc(dt_trans, 1)

            def turn_v(i):
                pe.wait_ge(vst_ready, i + 1)
                if isinstance(i, int) and i == 0:
                    pe.wait_ge(sst_done, 2)
                else:
                    pe.wait_ge(vtok_ready, i)
                for n in range(2):
                    last = pe.transpose(ps[0:VNEW, 5, n * P:(n + 1) * P], vst[:, n, :], ident[:])
                last.then_inc(vt_done, 1)

            def glu(i):
                first = isinstance(i, int) and i == 0
                for p in range(2):
                    if first:
                        pe.wait_ge(x_copied, NT)
                    elif p == 0:
                        pe.wait_ge(read_act, i)
                    else:
                        pe.wait_ge(read_dve, i)
                    for kq in range(4):
                        granule(Q_GLU + 2 * i + p, kq, 2 * p, ahi, alo)
                        c = 4 * p + kq
                        if first:
                            turn_conv_states(c)
                        if first and c in (2, 4):
                            turn_xconv_states(c // 2 - 1)
                        if first and c == 6:
                            turn_dt()
                        if not first and p == 1 and kq == 0:
                            turn_v(i - 1)

            glu(0)
            with pe.Fori(1, 8) as i:
                glu(i)

            def turn_xw(i):
                pe.wait_ge(xw_ready, 2 * i + 2)
                if isinstance(i, int) and i == 0:
                    pe.wait_ge(vtok_ready, 8)
                else:
                    pe.wait_ge(xtok_ready, i)
                for p in range(2):
                    for n in range(2):
                        last = pe.transpose(ps[0:XNEW, 5, (2 * p + n) * P:(2 * p + n + 1) * P], xw[:, p, n, :],
                                            ident[:])
                last.then_inc(xwt_done, 1)

            def xbc(i):
                first = isinstance(i, int) and i == 0
                for p in range(2):
                    if first:
                        pe.wait_ge(*((read_act, 8) if p == 0 else (read_dve, 8)))
                    else:
                        pe.wait_ge(read_act, 8 + 2 * i + p - 1)
                    for kq in range(4):
                        granule(Q_XBC + 2 * i + p, kq, 2 * p, ahi, alo)
                        if p == 1 and kq == 0:
                            turn_v(7) if first else turn_xw(i - 1)

            xbc(0)
            with pe.Fori(1, 6) as i:
                xbc(i)

            def z(i, tail=False):
                for p in range(2):
                    pe.wait_ge(read_act, 20 + 2 * i + p - 1)
                    for kq in range(4):
                        granule(Q_Z + 2 * i + p, kq, 2 * p, ahi, alo)
                        if isinstance(i, int) and i == 0 and p == 1 and kq == 0:
                            turn_xw(5)
                        if tail and p == 0 and kq == 0:
                            pe.wait_ge(msum_done, 1)
                            pe.wait_ge(dt_ready, 1)
                            pe.matmul(ps[:, 4, 0:TOK], mean1[:], msum[:], start=True, stop=True
                                      ).then_inc(mean_mm, 1)
                        if tail and p == 1:
                            pe.wait_ge(sq_summed, kq + 1)
                            if kq == 0:
                                pe.wait_ge(mean_done, 1)
                            pe.matmul(ps[:, 4, 0:TOK], mean1[:], sqs[:], start=(kq == 0), stop=(kq == 3)
                                      ).then_inc(sq_used, 1)

            z(0)
            with pe.Fori(1, 3) as i:
                z(i)
            z(3, tail=True)

            def scan_front(i, j):
                T = 4 * i + j
                first = isinstance(i, int) and i == 0 and j == 0
                if j == 0:
                    pe.wait_ge(bt_ready, i + 1)
                    if not first:
                        pe.wait_ge(pst_done, T)
                        pe.wait_ge(hts_ready, T)
                        pe.wait_ge(mixw_done, 2 * T)
                    else:
                        pe.wait_ge(var_root, 1)
                        pe.wait_ge(read_act, 28)
                    for c, off in enumerate((0, P, TOK - P)):
                        last = pe.transpose(ps[:, 4, c * P:(c + 1) * P], bt[:, off:off + P], ident[:])
                    last.then_inc(bt_trans, 1)
                    for c, off in enumerate((0, P, TOK - P)):
                        hi = min((c + 1) * P, TOK)
                        last = pe.matmul(ps[:, 2, c * P:hi], bt[:, off:off + P], xb[:, NT + GROUPS + i, c * P:hi],
                                         start=True, stop=True)
                    last.then_inc(cb_done, 1)
                    pe.wait_ge(btok_ready, i + 1)
                else:
                    pe.wait_ge(pst_done, T)
                pe.wait_ge(xst_ready, T + 1)
                for c, off in enumerate((0, P, TOK - P)):
                    last = pe.transpose(ps[:, 4, c * P:(c + 1) * P], xst[:, off:off + P], ident[:])
                last.then_inc(xtile_trans, 1)
                segment(T, 0, first)
                pe.wait_ge(h0_in[j % 2], 16 * (2 * i + j // 2 + 1))
                if not first:
                    pe.wait_ge(hnew_done, T)
                for b in range(NB):
                    last = pe.transpose(ps[:, 6 + b // 4, (b % 4) * P:(b % 4 + 1) * P], h0[:, j % 2, b, :],
                                        ident[:])
                last.then_inc(h0_trans, 1)

            def segment(T, e, first):
                if not (first and e == 0):
                    pe.wait_ge(exp_done, 2 * T + e)
                seg = ps[:, 3, 0:TOK]
                pe.matmul(seg, identb[:], mneg[:], start=True, stop=False)
                pe.matmul(seg, sel[:, ds(2 * T + e, 1)].to_broadcast([P, P]), cum3[:], start=False, stop=False)
                for c, off in enumerate((0, P, TOK - P)):
                    lo, hi = c * P, min((c + 1) * P, TOK)
                    last = pe.matmul(ps[:, 3, lo:hi], cum3[:, off:off + P],
                                     nsel[:, ds(2 * T + e, 1)].to_broadcast([P, hi - lo]), start=False, stop=(c == 2))
                last.then_inc(seg_done, 1)

            def within(T, e):
                for c in range(3):
                    lo, hi = c * P, min((c + 1) * P, TOK)
                    last = pe.matmul(ps[e * HD:(e + 1) * HD, 5, lo:hi], xd[:, c, e * HD:(e + 1) * HD],
                                     wgt[:, e, lo:hi], start=True, stop=True)
                return last

            def scan_back(i, j):
                T = 4 * i + j
                first = isinstance(i, int) and i == 0 and j == 0
                segment(T, 1, first)
                if not first:
                    pe.wait_ge(ecb_ready, T)
                pe.wait_ge(selt_ready, T + 1)
                pe.wait_ge(mixw_done, 2 * T + 1)
                pe.matmul(ps[:, 2, TOK:512], selt[:].rearrange("p h d -> p (h d)"),
                          ecum3[:, P:TOK], start=True, stop=True).then_inc(ecb_mm, 1)
                pe.wait_ge(xd_ready, T + 1)
                pe.wait_ge(btok_ready, i + 1)
                pe.matmul(ps[:, 4, 384:512], btok[:, 0, :], xdd[:, 0, :], start=True, stop=True
                          ).then_inc(pstart_done, 1)
                if not first:
                    pe.wait_ge(y_read, T)
                within(T, 0)
                pe.wait_ge(h0t_ready, T + 1)
                for b in range(NB):
                    pe.matmul(ps[:, 5, 448 + DS * b:456 + DS * b], h0t[:, b, :],
                              xb[:, NT + GROUPS + i, SEQ + DS * b:SEQ + DS * (b + 1)], start=True, stop=True)
                pe.wait_ge(hts_ready, T + 1)
                pe.matmul(ps[:, 5, TOK:448], hts[:], xb[:, NT + GROUPS + i, P:SEQ], start=True, stop=True)
                for c in range(2):
                    pe.matmul(ps[:, 4, c * P:(c + 1) * P], xdd[:, c, :], btok[:, c, :], start=True, stop=True)
                pe.wait_ge(bm_ready, i + 1)
                for h in range(2):
                    last = pe.matmul(ps[:, 6 + h, :], xdd[:, 2, :], bm[:, 4 * h:4 * h + 4, :], start=True, stop=True)
                last.then_inc(st_done, 1)
                pe.wait_ge(mixw_done, 2 * T + 2)
                within(T, 1).then_inc(y_done, 1)

            def wc(i):
                first = isinstance(i, int) and i == 0
                for j in range(4):
                    p, kq = j // 2, 2 * (j % 2)
                    if first and j < 2:
                        pe.wait_ge(act_ready, NT + 4 * kq + 4)
                    if kq == 0:
                        pe.wait_ge(read_act, 28 + 2 * i + p)
                    granule(Q_WC + 2 * i + p, kq, 0, ahi, alo)
                    scan_front(i, j)
                    if first and j < 2:
                        pe.wait_ge(act_ready, NT + 4 * kq + 8)
                    granule(Q_WC + 2 * i + p, kq + 1, 0, ahi, alo)
                    scan_back(i, j)

            wc(0)
            with pe.Fori(1, 4) as i:
                wc(i)

            pe.wait_ge(gss_done, 1)
            pe.wait_ge(y_read, NT)
            pe.wait_ge(pst_done, NT)
            pe.wait_ge(mixw_done, 2 * NT)
            for g in range(GROUPS):
                last = pe.matmul(ps[:, 2 + g, 0:TOK], mean1[:], gss[:, g, :], start=True, stop=True)
            last.then_inc(gn_mm, 1)

            def gemm(pair0, i, hi, lo, counts, operand=None):
                for p in range(2):
                    for s, v in counts(p):
                        pe.wait_ge(s, v)
                    for kq in range(4):
                        if operand and p == 0:
                            pe.wait_ge(operand[0], operand[1] + operand[2] * (kq + 1))
                        granule(pair0 + 2 * i + p, kq, 2 * p, hi, lo)

            gemm(Q_WS, 0, ahi, alo, lambda p: [(read_act, 36), (gn_root, GROUPS)], (act_ready, 2 * NT, 4))
            with pe.Fori(1, 4) as i:
                gemm(Q_WS, i, ahi, alo, lambda p: [(read_dve, 8 + 2 * i + p - 1)])

            pe.wait_ge(acc_done, 1)
            for n in range(2):
                last = pe.matmul(ps[:, 4, 0:TOK], mean1[:], acc2[:, n, :], start=(n == 0), stop=(n == 1))
            last.then_inc(rms_mm, 1)

            def rms_x1():
                pe.wait_ge(acc_done, 2)
                for n in range(2):
                    last = pe.matmul(ps[:, 5, 0:TOK], mean1[:], acc2[:, n, :], start=(n == 0), stop=(n == 1))
                last.then_inc(rms_mm, 1)

            def up0(q, counts):
                gemm(q_up(q), 0, ahi, alo, counts)

            for p in range(2):
                pe.wait_ge(read_dve, 15 + p)
                for kq in range(4):
                    if p == 0:
                        pe.wait_ge(act_ready, 3 * NT + 4 * (kq + 1))
                    granule(q_up(0) + p, kq, 2 * p, ahi, alo)
                    if p == 0 and kq == 0:
                        rms_x1()
            with pe.Fori(1, 4) as i:
                gemm(q_up(0), i, ahi, alo, lambda p: [(rh_done, 2 * i + p - 1)])
            gemm(q_down(0), 0, hhi, hlo, lambda p: [(rh_done, 7 + p)], (hid_ready, 0, 2))
            with pe.Fori(1, 4) as i:
                gemm(q_down(0), i, hhi, hlo, lambda p: [(read_act, 36 + 2 * i + p - 1)])

            def quarter(q, last_read):
                gemm(q_up(q), 0, ahi, alo, last_read)
                with pe.Fori(1, 4) as i:
                    gemm(q_up(q), i, ahi, alo, lambda p: [(rh_done, 8 * q + 2 * i + p - 1)])
                gemm(q_down(q), 0, hhi, hlo, lambda p: [(rh_done, 8 * q + 7 + p)], (hid_ready, 8 * q, 2))
                with pe.Fori(1, 4) as i:
                    gemm(q_down(q), i, hhi, hlo, lambda p: [(read_dve, 8 + 8 * q + 2 * i + p - 1)])

            quarter(1, lambda p: [(read_act, 43 + p)])
            with pe.Fori(2, 4) as q:
                quarter(q, lambda p: [(read_dve, 8 + 8 * q - 1 + p)])

            pe.wait_ge(acc_done, 3)
            for n in range(2):
                last = pe.matmul(ps[:, 4, 0:TOK], mean1[:], acc2[:, n, :], start=(n == 0), stop=(n == 1))
            last.then_inc(rms_mm, 1)
            pe.wait_ge(rms_done, 3)
            for g in range(4):
                pe.wait_ge(x1_done, NT + 4 * g + 4)
                if g >= 2:
                    pe.wait_ge(ot_copied, g - 1)
                b = 3 * (g % 2)
                for n in range(4):
                    t, cols = 4 * g + n, slice(n * P, (n + 1) * P)
                    pe.transpose(ps[:, b, cols], mix[:, t, 0:P], ident[:])
                    pe.transpose(ps[:, b + 1, cols], mix[:, t, P:SEQ], ident[:])
                    last = pe.transpose(ps[0:64, b + 2, cols], mix[:, t, SEQ:TOK], ident[:])
                last.then_inc(ot_trans, 1)


_INS = ["x_prompt", "x_sample", "state_ssm", "state_ssd_conv", "state_conformer_conv", "w_in", "ssd_conv_w",
        "ssd_conv_b", "dt_bias", "a_log", "d_skip", "ssd_norm_w", "conf_conv_w", "conf_conv_b", "conf_norm_w",
        "conf_norm_b", "w_out", "norm_pre_mix", "norm_post_mix", "norm_pre_mlp", "norm_post_mlp", "w_up",
        "w_down"]
_OUTS = [(1, SEQ, D), (NB, DS, D), (1, 1, HEADS, HD, STATE), (1, 1, XHALO, D_XBC), (1, 1, HALO, D),
         (1, NB, HEADS, HD, STATE), (1, NB, XHALO, D_XBC), (1, NB, HALO, D)]


def kernel(**inputs):
    import concourse.bacc as bacc
    from concourse.bass_utils import run_bass_kernel_spmd as run

    nc = bacc.Bacc("TRN2", target_bir_lowering=False, num_devices=1)
    arrays, args = {}, []
    for name in _INS:
        a = np.ascontiguousarray(inputs[name])
        arrays[f"in_{name}"] = a
        args.append(nc.dram_tensor(f"in_{name}", a.shape, mybir.dt.from_np(a.dtype), kind="ExternalInput").ap())
    for i, shape in enumerate(_OUTS):
        args.append(nc.dram_tensor(f"out_{i}", shape, F32, kind="ExternalOutput").ap())
    args.append(nc.dram_tensor("x_transposed", (P, NT * TOK), F32, kind="Internal").ap())
    build(nc, *args)
    r = run(nc, [arrays], core_ids=[0])
    return tuple(r.results[0][f"out_{i}"] for i in range(len(_OUTS)))
```
